# Optimizing a Trainium2 kernel written in Bass

```python
import math
import jax
import jax.numpy as jnp
from jax import lax
import numpy as np
import jax, jax.numpy as jnp

D_MODEL = 1024
BATCH = 1
SEQ = 512
DEPTH = 2

GRID_W = 64
CTX_LEN = 256
N_MIXERS = 3
D_FF = 4 * D_MODEL
NORM_EPS = 1e-6
ROPE_BASE = 10000.0

A_HEADS = 8
A_DQK = D_MODEL // (2 * A_HEADS)
A_DV = D_MODEL // A_HEADS
A_CHUNK = 128
A_IN = 2 * A_HEADS * A_DQK + A_HEADS * A_DV + D_MODEL + 4 * A_HEADS

SWA_HEADS = 16
SWA_KV_HEADS = 4
SWA_DH = D_MODEL // SWA_HEADS
SWA_GROUP = SWA_HEADS // SWA_KV_HEADS
WINDOW = 128
SWA_BLOCK = WINDOW
SWA_IN = (SWA_HEADS + 2 * SWA_KV_HEADS) * SWA_DH

DIFF_HEADS = 8
DIFF_DH = D_MODEL // (2 * DIFF_HEADS)
DIFF_DV = 2 * DIFF_DH
DIFF_BLOCK = 128
DIFF_IN = 4 * DIFF_HEADS * DIFF_DH + DIFF_HEADS * DIFF_DV

N_MLSTM = (DEPTH + N_MIXERS - 1) // N_MIXERS
N_SWA = (DEPTH + N_MIXERS - 2) // N_MIXERS
N_DIFF = (DEPTH + N_MIXERS - 3) // N_MIXERS


F32 = jnp.float32

def _rms_norm(x, g):
    xf = x.astype(F32)
    y = xf * lax.rsqrt(jnp.mean(xf * xf, axis=-1, keepdims=True) + NORM_EPS)
    return (y * g.astype(F32)).astype(x.dtype)

def _modulate(x, shift, scale):
    return x * (1.0 + scale) + shift

def _sq_relu_mlp(u, w1, w2):
    return jnp.square(jax.nn.relu(u @ w1)) @ w2

def _axial_rope_tables(n_tok, head_dim):
    rows = n_tok // GRID_W
    row = jnp.repeat(jnp.arange(rows, dtype=jnp.int32), GRID_W).astype(F32)
    col = jnp.tile(jnp.arange(GRID_W, dtype=jnp.int32), rows).astype(F32)
    quarter = head_dim // 4
    inv = ROPE_BASE ** (-jnp.arange(quarter, dtype=F32) / quarter)
    ang = jnp.concatenate([row[:, None] * inv, col[:, None] * inv], axis=-1)
    return jnp.cos(ang), jnp.sin(ang)

def _apply_rope(x, cos, sin):
    half = x.shape[-1] // 2
    x1, x2 = x[..., :half], x[..., half:]
    cs = cos[:, None, :].astype(x.dtype)
    sn = sin[:, None, :].astype(x.dtype)
    return jnp.concatenate([x1 * cs - x2 * sn, x1 * sn + x2 * cs], axis=-1)

def _to_chunks(t):
    bsz, n, h = t.shape[:3]
    t = t.reshape((bsz, n // A_CHUNK, A_CHUNK, h) + t.shape[3:])
    return jnp.moveaxis(t, 3, 1)

def _from_chunks(t):
    t = jnp.moveaxis(t, 1, 3)
    return t.reshape((t.shape[0], t.shape[1] * t.shape[2]) + t.shape[3:])

def _mlstm_direction(q, k, v, log_i, log_f, state, need_out):
    k_c, v_c = _to_chunks(k), _to_chunks(v)
    li, lf = _to_chunks(log_i), _to_chunks(log_f)
    b = jnp.cumsum(lf, axis=-1)
    b_last = b[..., -1]
    a = b_last[..., None] - b + li
    g = jnp.max(a, axis=-1)
    w = jnp.exp(a - g[..., None])
    kv = jnp.einsum("bhcs,bhcsd,bhcse->bhcde", w, k_c, v_c)
    kn = jnp.einsum("bhcs,bhcsd->bhcd", w, k_c)

    def step(carry, xs):
        c_st, n_st, m_st = carry
        bl, gj, kvj, knj = xs
        m_new = jnp.maximum(bl + m_st, gj)
        decay = jnp.exp(bl + m_st - m_new)
        inject = jnp.exp(gj - m_new)
        c_new = decay[..., None, None] * c_st + inject[..., None, None] * kvj
        n_new = decay[..., None] * n_st + inject[..., None] * knj
        return (c_new, n_new, m_new), (c_st, n_st, m_st)

    xs = (jnp.moveaxis(b_last, 2, 0), jnp.moveaxis(g, 2, 0), jnp.moveaxis(kv, 2, 0), jnp.moveaxis(kn, 2, 0))
    final, starts = lax.scan(step, state, xs)
    if not need_out:
        return None, final
    c0 = jnp.moveaxis(starts[0], 0, 2)
    n0 = jnp.moveaxis(starts[1], 0, 2)
    m0 = jnp.moveaxis(starts[2], 0, 2)
    q_c = _to_chunks(q)
    L = q_c.shape[-2]
    d = b[..., :, None] - b[..., None, :] + li[..., None, :]
    d = jnp.where(jnp.tril(jnp.ones((L, L), dtype=bool)), d, -jnp.inf)
    inter = b + m0[..., None]
    m_t = jnp.maximum(jnp.max(d, axis=-1), inter)
    wq = jnp.exp(d - m_t[..., None]) * jnp.einsum("bhctd,bhcsd->bhcts", q_c, k_c)
    carry_w = jnp.exp(inter - m_t)
    num = jnp.einsum("bhcts,bhcse->bhcte", wq, v_c) + carry_w[..., None] * jnp.einsum("bhctd,bhcde->bhcte", q_c, c0)
    den = jnp.sum(wq, axis=-1) + carry_w * jnp.einsum("bhctd,bhcd->bhct", q_c, n0)
    h = num / jnp.maximum(jnp.abs(den), jnp.exp(-m_t))[..., None]
    return _from_chunks(h), final

def _mlstm_mixer(u_ctx, u_lat, w_in, gate_b, head_norm, w_out, need_ctx):
    qk = A_HEADS * A_DQK
    vd = A_HEADS * A_DV
    splits = [qk, 2 * qk, 2 * qk + vd, 2 * qk + vd + D_MODEL]

    def project(u):
        bsz, n = u.shape[:2]
        q, k, v, o, gates = jnp.split(u @ w_in, splits, axis=-1)
        q = q.astype(F32).reshape(bsz, n, A_HEADS, A_DQK)
        k = k.astype(F32).reshape(bsz, n, A_HEADS, A_DQK) * (A_DQK ** -0.5)
        v = v.astype(F32).reshape(bsz, n, A_HEADS, A_DV)
        gates = gates.astype(F32).reshape(bsz, n, 4, A_HEADS) + gate_b.astype(F32)
        fwd = (gates[:, :, 0], jax.nn.log_sigmoid(gates[:, :, 1]))
        bwd = (gates[:, :, 2], jax.nn.log_sigmoid(gates[:, :, 3]))
        return q, k, v, o, fwd, bwd

    def flip(t):
        return jnp.flip(t, axis=1)

    cq, ck, cv, co, cf, cb = project(u_ctx)
    lq, lk, lv, lo, lf, lb = project(u_lat)
    bsz = u_lat.shape[0]
    zero = (jnp.zeros((bsz, A_HEADS, A_DQK, A_DV), F32), jnp.zeros((bsz, A_HEADS, A_DQK), F32),
            jnp.zeros((bsz, A_HEADS), F32))
    hcf, st_f = _mlstm_direction(cq, ck, cv, cf[0], cf[1], zero, need_ctx)
    hcb, st_b = _mlstm_direction(flip(cq), flip(ck), flip(cv), flip(cb[0]), flip(cb[1]), zero, need_ctx)
    hlf, _ = _mlstm_direction(lq, lk, lv, lf[0], lf[1], st_f, True)
    hlb, _ = _mlstm_direction(flip(lq), flip(lk), flip(lv), flip(lb[0]), flip(lb[1]), st_b, True)

    def finish(hf, hb, o):
        hs = hf + flip(hb)
        hn = hs * lax.rsqrt(jnp.mean(hs * hs, axis=-1, keepdims=True) + NORM_EPS)
        hn = hn * head_norm.astype(F32).reshape(A_HEADS, A_DV)
        bsz_, n = hs.shape[:2]
        return (hn.reshape(bsz_, n, vd).astype(o.dtype) * jax.nn.sigmoid(o)) @ w_out

    y_lat = finish(hlf, hlb, lo)
    y_ctx = finish(hcf, hcb, co) if need_ctx else None
    return y_lat, y_ctx

def _swa_mixer(u_ctx, u_lat, w_in, sink, w_out, cos, sin, need_ctx):
    scale = SWA_DH ** -0.5
    sink_g = sink.astype(F32).reshape(SWA_KV_HEADS, SWA_GROUP)[:, :, None]

    def project(u):
        bsz, n = u.shape[:2]
        q, k, v = jnp.split(u @ w_in, [SWA_HEADS * SWA_DH, (SWA_HEADS + SWA_KV_HEADS) * SWA_DH], axis=-1)
        return (q.reshape(bsz, n, SWA_HEADS, SWA_DH), k.reshape(bsz, n, SWA_KV_HEADS, SWA_DH),
                v.reshape(bsz, n, SWA_KV_HEADS, SWA_DH))

    cq, ck, cv = project(u_ctx)
    lq, lk, lv = project(u_lat)
    lq = _apply_rope(lq, cos, sin)
    lk = _apply_rope(lk, cos, sin)
    bsz, n_tok = u_lat.shape[:2]
    nb = n_tok // SWA_BLOCK
    kp = jnp.pad(lk, ((0, 0), (SWA_BLOCK, SWA_BLOCK), (0, 0), (0, 0)))
    vp = jnp.pad(lv, ((0, 0), (SWA_BLOCK, SWA_BLOCK), (0, 0), (0, 0)))
    q_blocks = jnp.moveaxis(lq.reshape(bsz, nb, SWA_BLOCK, SWA_KV_HEADS, SWA_GROUP, SWA_DH), 1, 0)
    q_idx = jnp.arange(SWA_BLOCK)[:, None]
    k_idx = jnp.arange(3 * SWA_BLOCK)[None, :]
    rel = k_idx - SWA_BLOCK - q_idx

    def block(args):
        j, qb = args
        kb = lax.dynamic_slice_in_dim(kp, j * SWA_BLOCK, 3 * SWA_BLOCK, axis=1)
        vb = lax.dynamic_slice_in_dim(vp, j * SWA_BLOCK, 3 * SWA_BLOCK, axis=1)
        kpos = j * SWA_BLOCK - SWA_BLOCK + k_idx
        valid = (jnp.abs(rel) <= WINDOW) & (kpos >= 0) & (kpos < n_tok)
        s_lat = jnp.einsum("bqhgd,bkhd->bhgqk", qb, kb).astype(F32) * scale
        s_lat = jnp.where(valid, s_lat, -jnp.inf)
        s_ctx = jnp.einsum("bqhgd,bchd->bhgqc", qb, ck).astype(F32) * scale
        m = jnp.maximum(jnp.maximum(jnp.max(s_lat, -1), jnp.max(s_ctx, -1)), sink_g)
        p_lat = jnp.exp(s_lat - m[..., None])
        p_ctx = jnp.exp(s_ctx - m[..., None])
        den = jnp.sum(p_lat, -1) + jnp.sum(p_ctx, -1) + jnp.exp(sink_g - m)
        o = jnp.einsum("bhgqk,bkhd->bqhgd", p_lat, vb) + jnp.einsum("bhgqc,bchd->bqhgd", p_ctx, cv)
        return o / jnp.moveaxis(den, 3, 1)[..., None]

    o_lat = lax.map(block, (jnp.arange(nb), q_blocks))
    o_lat = jnp.moveaxis(o_lat, 0, 1).reshape(bsz, n_tok, SWA_HEADS * SWA_DH)
    y_lat = o_lat.astype(u_lat.dtype) @ w_out
    if not need_ctx:
        return y_lat, None
    n_ctx = u_ctx.shape[1]
    cqg = cq.reshape(bsz, n_ctx, SWA_KV_HEADS, SWA_GROUP, SWA_DH)
    s = jnp.einsum("bqhgd,bchd->bhgqc", cqg, ck).astype(F32) * scale
    m = jnp.maximum(jnp.max(s, -1), sink_g)
    p = jnp.exp(s - m[..., None])
    den = jnp.sum(p, -1) + jnp.exp(sink_g - m)
    o_ctx = jnp.einsum("bhgqc,bchd->bqhgd", p, cv) / jnp.moveaxis(den, 3, 1)[..., None]
    y_ctx = o_ctx.reshape(bsz, n_ctx, SWA_HEADS * SWA_DH).astype(u_ctx.dtype) @ w_out
    return y_lat, y_ctx

def _diff_mixer(u_ctx, u_lat, w_in, lam_q1, lam_k1, lam_q2, lam_k2, head_norm, w_out, cos, sin,
                layer_idx, need_ctx):
    scale = DIFF_DH ** -0.5
    lam_init = 0.8 - 0.6 * math.exp(-0.3 * layer_idx)
    lam = (jnp.exp(jnp.sum(lam_q1.astype(F32) * lam_k1.astype(F32)))
           - jnp.exp(jnp.sum(lam_q2.astype(F32) * lam_k2.astype(F32))) + lam_init)
    qk = 2 * DIFF_HEADS * DIFF_DH

    def project(u, rope):
        bsz, n = u.shape[:2]
        q, k, v = jnp.split(u @ w_in, [qk, 2 * qk], axis=-1)
        q = q.reshape(bsz, n, 2 * DIFF_HEADS, DIFF_DH)
        k = k.reshape(bsz, n, 2 * DIFF_HEADS, DIFF_DH)
        if rope:
            q = _apply_rope(q, cos, sin)
            k = _apply_rope(k, cos, sin)
        return (q.reshape(bsz, n, DIFF_HEADS, 2, DIFF_DH), k.reshape(bsz, n, DIFF_HEADS, 2, DIFF_DH),
                v.reshape(bsz, n, DIFF_HEADS, DIFF_DV))

    def finish(o, dtype):
        od = o[:, :, :, 0] - lam * o[:, :, :, 1]
        od = od * lax.rsqrt(jnp.mean(od * od, axis=-1, keepdims=True) + NORM_EPS)
        od = od * head_norm.astype(F32).reshape(DIFF_HEADS, DIFF_DV) * (1.0 - lam_init)
        bsz, n = od.shape[:2]
        return od.reshape(bsz, n, DIFF_HEADS * DIFF_DV).astype(dtype) @ w_out

    cq, ck, cv = project(u_ctx, False)
    lq, lk, lv = project(u_lat, True)
    bsz, n_tok = u_lat.shape[:2]
    nb = n_tok // DIFF_BLOCK
    q_blocks = jnp.moveaxis(lq.reshape(bsz, nb, DIFF_BLOCK, DIFF_HEADS, 2, DIFF_DH), 1, 0)

    def block(qb):
        s_lat = jnp.einsum("bqhmd,bkhmd->bhmqk", qb, lk).astype(F32) * scale
        s_ctx = jnp.einsum("bqhmd,bchmd->bhmqc", qb, ck).astype(F32) * scale
        mx = jnp.maximum(jnp.max(s_lat, -1), jnp.max(s_ctx, -1))[..., None]
        p_lat = jnp.exp(s_lat - mx)
        p_ctx = jnp.exp(s_ctx - mx)
        den = jnp.sum(p_lat, -1) + jnp.sum(p_ctx, -1)
        o = jnp.einsum("bhmqk,bkhe->bqhme", p_lat, lv) + jnp.einsum("bhmqc,bche->bqhme", p_ctx, cv)
        return o / jnp.moveaxis(den, 3, 1)[..., None]

    o_lat = lax.map(block, q_blocks)
    o_lat = jnp.moveaxis(o_lat, 0, 1).reshape(bsz, n_tok, DIFF_HEADS, 2, DIFF_DV)
    y_lat = finish(o_lat, u_lat.dtype)
    if not need_ctx:
        return y_lat, None
    s = jnp.einsum("bqhmd,bkhmd->bhmqk", cq, ck).astype(F32) * scale
    a = jax.nn.softmax(s, axis=-1)
    o_ctx = jnp.einsum("bhmqk,bkhe->bqhme", a, cv)
    return y_lat, finish(o_ctx, u_ctx.dtype)

def first_inputs(seed: int = 0) -> dict:
    key = jax.random.key(seed)
    ks = jax.random.split(key, 25)
    D = D_MODEL

    def nrm(k, shape, scale):
        return jax.random.normal(k, shape, F32) * scale

    forget_bias = jnp.linspace(3.0, 6.0, A_HEADS, dtype=F32)
    zeros_h = jnp.zeros((A_HEADS,), F32)
    gate_base = jnp.stack([zeros_h, forget_bias, zeros_h, forget_bias])
    return {
        "x": nrm(ks[0], (BATCH, SEQ, D), 1.0),
        "c": nrm(ks[1], (BATCH, D), 1.0),
        "ctx": nrm(ks[2], (BATCH, CTX_LEN, D), 1.0),
        "c_ctx": nrm(ks[3], (D,), 1.0),
        "ada_w": nrm(ks[4], (DEPTH, D, 6 * D), 0.5 * D ** -0.5),
        "ada_b": nrm(ks[5], (DEPTH, 6 * D), 0.02),
        "norm_mix": 1.0 + nrm(ks[6], (DEPTH, D), 0.02),
        "norm_ffn": 1.0 + nrm(ks[7], (DEPTH, D), 0.02),
        "ffn_w1": nrm(ks[8], (DEPTH, D, D_FF), D ** -0.5),
        "ffn_w2": nrm(ks[9], (DEPTH, D_FF, D), D_FF ** -0.5),
        "mlstm_w_in": nrm(ks[10], (N_MLSTM, D, A_IN), D ** -0.5),
        "mlstm_gate_b": gate_base + nrm(ks[11], (N_MLSTM, 4, A_HEADS), 0.1),
        "mlstm_head_norm": 1.0 + nrm(ks[12], (N_MLSTM, A_HEADS * A_DV), 0.02),
        "mlstm_w_out": nrm(ks[13], (N_MLSTM, A_HEADS * A_DV, D), (A_HEADS * A_DV) ** -0.5),
        "swa_w_in": nrm(ks[14], (N_SWA, D, SWA_IN), D ** -0.5),
        "swa_sink": nrm(ks[15], (N_SWA, SWA_HEADS), 0.5),
        "swa_w_out": nrm(ks[16], (N_SWA, SWA_HEADS * SWA_DH, D), (SWA_HEADS * SWA_DH) ** -0.5),
        "diff_w_in": nrm(ks[17], (N_DIFF, D, DIFF_IN), D ** -0.5),
        "diff_lambda_q1": nrm(ks[18], (N_DIFF, DIFF_DH), 0.1),
        "diff_lambda_k1": nrm(ks[19], (N_DIFF, DIFF_DH), 0.1),
        "diff_lambda_q2": nrm(ks[20], (N_DIFF, DIFF_DH), 0.1),
        "diff_lambda_k2": nrm(ks[21], (N_DIFF, DIFF_DH), 0.1),
        "diff_head_norm": 1.0 + nrm(ks[22], (N_DIFF, DIFF_HEADS * DIFF_DV), 0.02),
        "diff_w_out": nrm(ks[23], (N_DIFF, DIFF_HEADS * DIFF_DV, D), (DIFF_HEADS * DIFF_DV) ** -0.5),
        "final_norm": 1.0 + nrm(ks[24], (D,), 0.02),
    }

def first_block(x, c, ctx, c_ctx, ada_w, ada_b, norm_mix, norm_ffn, ffn_w1, ffn_w2,
              mlstm_w_in, mlstm_gate_b, mlstm_head_norm, mlstm_w_out,
              swa_w_in, swa_sink, swa_w_out,
              diff_w_in, diff_lambda_q1, diff_lambda_k1, diff_lambda_q2, diff_lambda_k2,
              diff_head_norm, diff_w_out, final_norm):
    n_tok = x.shape[1]
    cos_s, sin_s = _axial_rope_tables(n_tok, SWA_DH)
    cos_d, sin_d = _axial_rope_tables(n_tok, DIFF_DH)
    cond_lat = jax.nn.silu(c)[:, None, :]
    cond_ctx = jax.nn.silu(c_ctx)[None, None, :]
    h, hc = x, ctx
    for i in range(DEPTH):
        kind, slot = i % N_MIXERS, i // N_MIXERS
        need_ctx = i < DEPTH - 1
        mod_l = jnp.split(cond_lat @ ada_w[i] + ada_b[i], 6, axis=-1)
        mod_c = jnp.split(cond_ctx @ ada_w[i] + ada_b[i], 6, axis=-1)
        u = _modulate(_rms_norm(h, norm_mix[i]), mod_l[0], mod_l[1])
        uc = _modulate(_rms_norm(hc, norm_mix[i]), mod_c[0], mod_c[1])
        if kind == 0:
            y, yc = _mlstm_mixer(uc, u, mlstm_w_in[slot], mlstm_gate_b[slot], mlstm_head_norm[slot],
                                 mlstm_w_out[slot], need_ctx)
        elif kind == 1:
            y, yc = _swa_mixer(uc, u, swa_w_in[slot], swa_sink[slot], swa_w_out[slot], cos_s, sin_s, need_ctx)
        else:
            y, yc = _diff_mixer(uc, u, diff_w_in[slot], diff_lambda_q1[slot], diff_lambda_k1[slot],
                                diff_lambda_q2[slot], diff_lambda_k2[slot], diff_head_norm[slot],
                                diff_w_out[slot], cos_d, sin_d, i, need_ctx)
        h = h + mod_l[2] * y
        h = h + mod_l[5] * _sq_relu_mlp(_modulate(_rms_norm(h, norm_ffn[i]), mod_l[3], mod_l[4]),
                                        ffn_w1[i], ffn_w2[i])
        if need_ctx:
            hc = hc + mod_c[2] * yc
            hc = hc + mod_c[5] * _sq_relu_mlp(_modulate(_rms_norm(hc, norm_ffn[i]), mod_c[3], mod_c[4]),
                                              ffn_w1[i], ffn_w2[i])
    return _rms_norm(h, final_norm)


ATTN_HEAD_DIM = 64
ATTN_HEADS = 8
ATTN_KV_HEADS = 2
ATTN_Q_PER_KV = ATTN_HEADS // ATTN_KV_HEADS
ATTN_WIDTH = ATTN_HEADS * ATTN_HEAD_DIM
ATTN_KV_WIDTH = ATTN_KV_HEADS * ATTN_HEAD_DIM
Q_BLOCK = 128
ROPE_THETA = 10000.0
ROPE_AXIS_DIM = ATTN_HEAD_DIM // 2

GLA_HEADS = 4
GLA_DK = 64
GLA_DV = 128
GLA_K_WIDTH = GLA_HEADS * GLA_DK
GLA_V_WIDTH = GLA_HEADS * GLA_DV
GLA_GATE_RANK = 16
GLA_GATE_TEMP = 16.0
GLA_CHUNK = 64

SGU_GROUPS = 4
SGU_CHUNK = 128
SGU_WIDTH = 512
SGU_GROUP_DIM = SGU_WIDTH // SGU_GROUPS

DEEPNORM_ALPHA = (2 * DEPTH) ** 0.25
DEEPNORM_BETA = (8 * DEPTH) ** -0.25
EPS = 1e-6

SPLIT_SIZES = (
    ATTN_WIDTH, ATTN_KV_WIDTH, ATTN_KV_WIDTH, ATTN_WIDTH,
    GLA_K_WIDTH, GLA_K_WIDTH, GLA_V_WIDTH, GLA_GATE_RANK, GLA_GATE_RANK,
    GLA_V_WIDTH,
    SGU_WIDTH, SGU_WIDTH, SGU_WIDTH,
    D_MODEL, D_MODEL, D_MODEL,
)
PROJ_WIDTH = sum(SPLIT_SIZES)


def _split_points():
    pts, acc = [], 0
    for s in SPLIT_SIZES[:-1]:
        acc += s
        pts.append(acc)
    return pts

def layer_norm(x, g, b):
    xf = x.astype(jnp.float32)
    mu = jnp.mean(xf, axis=-1, keepdims=True)
    var = jnp.mean(jnp.square(xf - mu), axis=-1, keepdims=True)
    return ((xf - mu) * lax.rsqrt(var + EPS) * g + b).astype(x.dtype)

def rms_norm(x, g):
    xf = x.astype(jnp.float32)
    y = xf * lax.rsqrt(jnp.mean(jnp.square(xf), axis=-1, keepdims=True) + EPS)
    return (y * g).astype(x.dtype)

def axial_rope_angles(rows):
    row = jnp.repeat(jnp.arange(rows, dtype=jnp.float32), GRID_W)
    col = jnp.tile(jnp.arange(GRID_W, dtype=jnp.float32), rows)
    freqs = ROPE_THETA ** (-jnp.arange(0, ROPE_AXIS_DIM, 2, dtype=jnp.float32) / ROPE_AXIS_DIM)
    return row[:, None] * freqs, col[:, None] * freqs

def rope_1d(x, ang):
    m = ang.shape[-1]
    cos = jnp.cos(ang)[None, :, None, :]
    sin = jnp.sin(ang)[None, :, None, :]
    x1, x2 = x[..., :m], x[..., m:]
    return jnp.concatenate([x1 * cos - x2 * sin, x1 * sin + x2 * cos], axis=-1)

def apply_axial_rope(x, ang_r, ang_c):
    xf = x.astype(jnp.float32)
    out = jnp.concatenate([rope_1d(xf[..., :ROPE_AXIS_DIM], ang_r),
                           rope_1d(xf[..., ROPE_AXIS_DIM:], ang_c)], axis=-1)
    return out.astype(x.dtype)

def gqa_project(pq, pk, pv, q_norm, k_norm):
    B, N, _ = pq.shape
    q = rms_norm(pq.reshape(B, N, ATTN_HEADS, ATTN_HEAD_DIM), q_norm)
    k = rms_norm(pk.reshape(B, N, ATTN_KV_HEADS, ATTN_HEAD_DIM), k_norm)
    v = pv.reshape(B, N, ATTN_KV_HEADS, ATTN_HEAD_DIM)
    return q, k, v

def attend(q, k, v):
    s = jnp.einsum('btgrd,blgd->bgrtl', q, k, preferred_element_type=jnp.float32) * (ATTN_HEAD_DIM ** -0.5)
    p = jax.nn.softmax(s, axis=-1)
    return jnp.einsum('bgrtl,blgd->btgrd', p.astype(v.dtype), v)

def blocked_attention(q, k, v):
    B, N = q.shape[:2]
    nb = N // Q_BLOCK
    qb = q.reshape(B, nb, Q_BLOCK, ATTN_KV_HEADS, ATTN_Q_PER_KV, ATTN_HEAD_DIM)
    qb = jnp.moveaxis(qb, 1, 0)
    ob = lax.map(lambda qi: attend(qi, k, v), qb)
    return jnp.moveaxis(ob, 0, 1).reshape(B, N, ATTN_WIDTH)

def gla_scan(q, k, v, g, s0):
    B, H, N, dk = q.shape
    dv = v.shape[-1]
    nc = N // GLA_CHUNK
    mask = jnp.tril(jnp.ones((GLA_CHUNK, GLA_CHUNK), dtype=bool))

    def chunks(t):
        return jnp.moveaxis(t.reshape(B, H, nc, GLA_CHUNK, t.shape[-1]), 2, 0)

    def step(s, inp):
        qc, kc, vc, gc = inp
        b = jnp.cumsum(gc, axis=2)
        b_last = b[:, :, -1:, :]
        inter = jnp.einsum('bhtd,bhde->bhte', qc * jnp.exp(b), s)
        rel = jnp.where(mask[:, :, None], b[:, :, :, None, :] - b[:, :, None, :, :], -jnp.inf)
        att = jnp.einsum('bhtd,bhsd,bhtsd->bhts', qc, kc, jnp.exp(rel))
        o = inter + jnp.einsum('bhts,bhse->bhte', att, vc)
        s_new = jnp.exp(b_last[:, :, 0, :])[..., None] * s + \
            jnp.einsum('bhsd,bhse->bhde', kc * jnp.exp(b_last - b), vc)
        return s_new, o

    s_fin, o = lax.scan(step, s0, (chunks(q), chunks(k), chunks(v), chunks(g)))
    return jnp.moveaxis(o, 0, 2).reshape(B, H, N, dv), s_fin

def gla_heads(pq, pk, pv, paf, pab, a2_f, ab_f, a2_b, ab_b):
    B, N, _ = pq.shape

    def heads(t, d):
        return t.reshape(B, N, GLA_HEADS, d).transpose(0, 2, 1, 3).astype(jnp.float32)

    def log_decay(pa, a2, ab):
        z = (pa @ a2 + ab).astype(jnp.float32)
        return heads(jax.nn.log_sigmoid(z) / GLA_GATE_TEMP, GLA_DK)

    q = heads(pq, GLA_DK) * (GLA_DK ** -0.5)
    k = heads(pk, GLA_DK)
    v = heads(pv, GLA_DV)
    return q, k, v, log_decay(paf, a2_f, ab_f), log_decay(pab, a2_b, ab_b)

def gla_finish(o, o_norm, dtype):
    B, H, N, dv = o.shape
    o = rms_norm(o.transpose(0, 2, 1, 3), o_norm)
    return o.reshape(B, N, H * dv).astype(dtype)

def sgu(pu, pv, ln_g, ln_b, w_s, b_s):
    B, N, _ = pu.shape
    nch = N // SGU_CHUNK
    vn = layer_norm(pv, ln_g, ln_b).reshape(B, nch, SGU_CHUNK, SGU_GROUPS, SGU_GROUP_DIM)
    mixed = jnp.einsum('gts,bnsgc->bntgc', w_s, vn) + b_s.T[None, None, :, :, None]
    return pu * mixed.reshape(B, N, SGU_WIDTH)

def trunk_layer(x, ctx, c, c_ctx, p, ang_r, ang_c, need_ctx):
    B = x.shape[0]
    shift, scale, gate = jnp.split(jax.nn.silu(c) @ p['w_ada'] + p['b_ada'], 3, axis=-1)
    shift_c, scale_c, gate_c = jnp.split(jax.nn.silu(c_ctx) @ p['w_ada'] + p['b_ada'], 3, axis=-1)
    h = x * (1.0 + scale[:, None, :]) + shift[:, None, :]
    hc = ctx * (1.0 + scale_c) + shift_c

    pts = _split_points()
    (a_q, a_k, a_v, a_g, g_q, g_k, g_v, g_af, g_ab, g_g,
     s_u, s_v, s_g, m_a, m_g, m_s) = jnp.split(h @ p['w_in'], pts, axis=-1)
    (ca_q, ca_k, ca_v, ca_g, cg_q, cg_k, cg_v, cg_af, cg_ab, cg_g,
     cs_u, cs_v, cs_g, cm_a, cm_g, cm_s) = jnp.split(hc @ p['w_in'], pts, axis=-1)

    ql, kl, vl = gqa_project(a_q, a_k, a_v, p['q_norm'], p['k_norm'])
    ql = apply_axial_rope(ql, ang_r, ang_c)
    kl = apply_axial_rope(kl, ang_r, ang_c)
    qc, kc, vc = gqa_project(ca_q, ca_k, ca_v, p['q_norm'], p['k_norm'])
    k_all = jnp.concatenate([kc, kl], axis=1)
    v_all = jnp.concatenate([vc, vl], axis=1)
    y_attn = blocked_attention(ql, k_all, v_all) * jax.nn.silu(a_g)

    qlg, klg, vlg, gfl, gbl = gla_heads(g_q, g_k, g_v, g_af, g_ab, p['a2_f'], p['ab_f'], p['a2_b'], p['ab_b'])
    qcg, kcg, vcg, gfc, gbc = gla_heads(cg_q, cg_k, cg_v, cg_af, cg_ab, p['a2_f'], p['ab_f'], p['a2_b'], p['ab_b'])
    zeros = jnp.zeros((B, GLA_HEADS, GLA_DK, GLA_DV), jnp.float32)
    flip = lambda t: jnp.flip(t, axis=2)
    oc_f, s_f = gla_scan(qcg, kcg, vcg, gfc, zeros)
    oc_b, s_b = gla_scan(flip(qcg), flip(kcg), flip(vcg), flip(gbc), zeros)
    ol_f, _ = gla_scan(qlg, klg, vlg, gfl, s_f)
    ol_b, _ = gla_scan(flip(qlg), flip(klg), flip(vlg), flip(gbl), s_b)
    y_gla = gla_finish(ol_f + flip(ol_b), p['gla_o_norm'], x.dtype) * jax.nn.silu(g_g)

    y_sgu = sgu(s_u, s_v, p['sgu_ln_g'], p['sgu_ln_b'], p['sgu_w'], p['sgu_b']) * jax.nn.silu(s_g)

    def merge(ya, yg, ys, ga, gg, gs):
        m = (jax.nn.sigmoid(ga) * (ya @ p['w_br_attn'])
             + jax.nn.sigmoid(gg) * (yg @ p['w_br_gla'])
             + jax.nn.sigmoid(gs) * (ys @ p['w_br_sgu']))
        return m @ p['w_out']

    out = merge(y_attn, y_gla, y_sgu, m_a, m_g, m_s)
    x_new = layer_norm(DEEPNORM_ALPHA * x + gate[:, None, :] * out, p['post_g'], p['post_b'])

    if not need_ctx:
        return x_new, ctx

    L = ctx.shape[1]
    yc_attn = attend(qc.reshape(B, L, ATTN_KV_HEADS, ATTN_Q_PER_KV, ATTN_HEAD_DIM), kc, vc)
    yc_attn = yc_attn.reshape(B, L, ATTN_WIDTH) * jax.nn.silu(ca_g)
    yc_gla = gla_finish(oc_f + flip(oc_b), p['gla_o_norm'], ctx.dtype) * jax.nn.silu(cg_g)
    yc_sgu = sgu(cs_u, cs_v, p['sgu_ln_g'], p['sgu_ln_b'], p['sgu_w'], p['sgu_b']) * jax.nn.silu(cs_g)
    out_c = merge(yc_attn, yc_gla, yc_sgu, cm_a, cm_g, cm_s)
    ctx_new = layer_norm(DEEPNORM_ALPHA * ctx + gate_c * out_c, p['post_g'], p['post_b'])
    return x_new, ctx_new

def second_inputs(seed: int = 0) -> dict:
    key = jax.random.key(seed)
    ks = iter(jax.random.split(key, 32))

    def nrm(shape, s):
        return jax.random.normal(next(ks), shape, jnp.float32) * s

    L, D = DEPTH, D_MODEL
    return {
        "x": nrm((BATCH, SEQ, D), 1.0),
        "c": nrm((BATCH, D), 1.0),
        "ctx": nrm((BATCH, CTX_LEN, D), 1.0),
        "c_ctx": nrm((D,), 1.0),
        "w_ada": nrm((L, D, 3 * D), 0.5 * D ** -0.5),
        "b_ada": nrm((L, 3 * D), 0.02),
        "w_in": nrm((L, D, PROJ_WIDTH), D ** -0.5),
        "attn_q_norm": 1.0 + nrm((L, ATTN_HEAD_DIM), 0.02),
        "attn_k_norm": 1.0 + nrm((L, ATTN_HEAD_DIM), 0.02),
        "gla_a2_f": nrm((L, GLA_GATE_RANK, GLA_K_WIDTH), GLA_GATE_RANK ** -0.5),
        "gla_ab_f": nrm((L, GLA_K_WIDTH), 0.1),
        "gla_a2_b": nrm((L, GLA_GATE_RANK, GLA_K_WIDTH), GLA_GATE_RANK ** -0.5),
        "gla_ab_b": nrm((L, GLA_K_WIDTH), 0.1),
        "gla_o_norm": 1.0 + nrm((L, GLA_DV), 0.02),
        "sgu_ln_g": 1.0 + nrm((L, SGU_WIDTH), 0.02),
        "sgu_ln_b": nrm((L, SGU_WIDTH), 0.02),
        "sgu_w": nrm((L, SGU_GROUPS, SGU_CHUNK, SGU_CHUNK), SGU_CHUNK ** -0.5),
        "sgu_b": 1.0 + nrm((L, SGU_GROUPS, SGU_CHUNK), 0.02),
        "w_br_attn": nrm((L, ATTN_WIDTH, D), ATTN_WIDTH ** -0.5 * DEEPNORM_BETA),
        "w_br_gla": nrm((L, GLA_V_WIDTH, D), GLA_V_WIDTH ** -0.5 * DEEPNORM_BETA),
        "w_br_sgu": nrm((L, SGU_WIDTH, D), SGU_WIDTH ** -0.5 * DEEPNORM_BETA),
        "w_out": nrm((L, D, D), D ** -0.5 * DEEPNORM_BETA),
        "post_ln_g": 1.0 + nrm((L, D), 0.02),
        "post_ln_b": nrm((L, D), 0.02),
    }

def second_block(x, c, ctx, c_ctx, w_ada, b_ada, w_in, attn_q_norm, attn_k_norm,
              gla_a2_f, gla_ab_f, gla_a2_b, gla_ab_b, gla_o_norm,
              sgu_ln_g, sgu_ln_b, sgu_w, sgu_b,
              w_br_attn, w_br_gla, w_br_sgu, w_out, post_ln_g, post_ln_b):
    n_lat = x.shape[1]
    rows = n_lat // GRID_W
    ang_r, ang_c = axial_rope_angles(rows)
    for i in range(DEPTH):
        p = {
            'w_ada': w_ada[i], 'b_ada': b_ada[i], 'w_in': w_in[i],
            'q_norm': attn_q_norm[i], 'k_norm': attn_k_norm[i],
            'a2_f': gla_a2_f[i], 'ab_f': gla_ab_f[i], 'a2_b': gla_a2_b[i], 'ab_b': gla_ab_b[i],
            'gla_o_norm': gla_o_norm[i],
            'sgu_ln_g': sgu_ln_g[i], 'sgu_ln_b': sgu_ln_b[i], 'sgu_w': sgu_w[i], 'sgu_b': sgu_b[i],
            'w_br_attn': w_br_attn[i], 'w_br_gla': w_br_gla[i], 'w_br_sgu': w_br_sgu[i],
            'w_out': w_out[i], 'post_g': post_ln_g[i], 'post_b': post_ln_b[i],
        }
        x, ctx = trunk_layer(x, ctx, c, c_ctx, p, ang_r, ang_c, need_ctx=(i < DEPTH - 1))
    return x


def setup_inputs(seed=0):
    out = dict(first_inputs(seed))
    for name, value in second_inputs(seed + 1).items():
        if name != "x":
            out[name + "_2"] = value
    return out


def reference(
    x, c, ctx, c_ctx, ada_w, ada_b, norm_mix, norm_ffn, ffn_w1, ffn_w2, mlstm_w_in,
    mlstm_gate_b, mlstm_head_norm, mlstm_w_out, swa_w_in, swa_sink, swa_w_out, diff_w_in,
    diff_lambda_q1, diff_lambda_k1, diff_lambda_q2, diff_lambda_k2, diff_head_norm, diff_w_out,
    final_norm, c_2, ctx_2, c_ctx_2, w_ada_2, b_ada_2, w_in_2, attn_q_norm_2, attn_k_norm_2,
    gla_a2_f_2, gla_ab_f_2, gla_a2_b_2, gla_ab_b_2, gla_o_norm_2, sgu_ln_g_2, sgu_ln_b_2,
    sgu_w_2, sgu_b_2, w_br_attn_2, w_br_gla_2, w_br_sgu_2, w_out_2, post_ln_g_2, post_ln_b_2,
):
    x = first_block(
        x, c, ctx, c_ctx, ada_w, ada_b, norm_mix, norm_ffn, ffn_w1, ffn_w2, mlstm_w_in,
        mlstm_gate_b, mlstm_head_norm, mlstm_w_out, swa_w_in, swa_sink, swa_w_out, diff_w_in,
        diff_lambda_q1, diff_lambda_k1, diff_lambda_q2, diff_lambda_k2, diff_head_norm,
        diff_w_out, final_norm,
    )
    return second_block(
        x, c_2, ctx_2, c_ctx_2, w_ada_2, b_ada_2, w_in_2, attn_q_norm_2, attn_k_norm_2,
        gla_a2_f_2, gla_ab_f_2, gla_a2_b_2, gla_ab_b_2, gla_o_norm_2, sgu_ln_g_2, sgu_ln_b_2,
        sgu_w_2, sgu_b_2, w_br_attn_2, w_br_gla_2, w_br_sgu_2, w_out_2, post_ln_g_2,
        post_ln_b_2,
    )


_drawn_inputs = setup_inputs


def setup_inputs(seed=0):
    import zlib

    import numpy as np

    out = dict(_drawn_inputs(seed))
    spreads = {}
    factors = {'norm_mix': 5.87,
     'norm_ffn': 4.463,
     'mlstm_head_norm': 8.0,
     'swa_sink': 8.0,
     'final_norm': 2.852,
     'ctx_2': 8.0,
     'c_ctx_2': 8.0,
     'b_ada_2': 8.0,
     'attn_q_norm_2': 8.0,
     'attn_k_norm_2': 8.0,
     'gla_a2_f_2': 8.0,
     'gla_ab_f_2': 8.0,
     'gla_a2_b_2': 8.0,
     'gla_ab_b_2': 23.745,
     'gla_o_norm_2': 64.0,
     'sgu_ln_g_2': 27.107,
     'sgu_ln_b_2': 24.789,
     'sgu_b_2': 27.276,
     'w_br_attn_2': 6.687}
    for name, (base, spread) in spreads.items():
        noise = np.random.default_rng([zlib.crc32(name.encode()), seed]).standard_normal(out[name].shape)
        drawn = base * np.exp(spread * noise) if base else spread * noise
        out[name] = jnp.asarray(drawn.astype(out[name].dtype))
    for name, factor in factors.items():
        out[name] = (out[name] * factor).astype(out[name].dtype)
    return out
```

```python
import math
from contextlib import ExitStack

import numpy as np
import concourse.bass as bass
from concourse import mybir

F32 = mybir.dt.float32
F32R = mybir.dt.float32r
U8 = mybir.dt.uint8
I32 = mybir.dt.int32
ALU = mybir.AluOpType
ACT = mybir.ActivationFunctionType
AX = mybir.AxisListType

D = 1024
LAT = 512
CTX = 256
TOK = LAT + CTX
EPS = 1e-6
ALPHA = 4 ** 0.25
NEG = -1e30

COLS = {}


def _layout():
    at = 0
    for name, n in [("ada_b0", 48), ("ada_b1", 48), ("ada2_b0", 24), ("ada2_b1", 24),
                    ("norm_mix0", 8), ("norm_mix1", 8), ("norm_ffn0", 8), ("norm_ffn1", 8),
                    ("head_norm", 8), ("final_norm", 8), ("post_g0", 8), ("post_g1", 8),
                    ("post_b0", 8), ("post_b1", 8), ("gla_o0", 1), ("gla_o1", 1),
                    ("abf0", 2), ("abf1", 2), ("abb0", 2), ("abb1", 2),
                    ("qn0", 1), ("qn1", 1), ("kn0", 1), ("kn1", 1), ("gb_i", 1), ("gb_f", 1),
                    ("cond", 32), ("sink", 16)]:
        COLS[name] = (at, n)
        at += n
    return at


NCOLS = _layout()


class Tok:

    def __init__(self, sem=None, value=0):
        self.sem, self.value, self.used = sem, value, False


class Prog:

    def __init__(self):
        self.q = {e: [] for e in ("pe", "act", "dve", "pool", "sp")}
        self.pending = {e: [] for e in self.q}
        self.newest = {}

    def op(self, e, fn, *waits):
        flat = []

        def walk(w):
            if w is None:
                return
            if isinstance(w, Tok):
                w.used = True
                flat.append(w)
            else:
                for x in w:
                    walk(x)
        walk(waits)
        walk(self.pending[e])
        self.pending[e] = []
        if e == "pool" and fn is not None:
            walk(self.newest.get("pool"))
        t = Tok(e)
        self.q[e].append((fn, flat, t, None))
        if fn is not None:
            self.newest[e] = t
        return t

    def dma(self, e, sem, out, in_, *waits):
        t0 = self.op(e, None, *waits)
        sem[1] += 16
        t = Tok(sem[0], sem[1])
        self.q[e][-1] = (lambda g, o=out, i=in_: g.dma_start(o, i), self.q[e][-1][1], t0, sem[0])
        return t

    def barrier(self, free=()):
        last = [t for e, t in self.newest.items() if e != "sp"]
        for e in self.q:
            if e != "sp" and e not in free:
                self.pending[e] = [t for t in last if t is not self.newest.get(e)] + [self.newest[e]] \
                    if e in self.newest else list(last)
        return last

    def emit(self, e, eng, sems):
        known = {}
        for fn, waits, t, dsem in self.q[e]:
            need = {}
            for w in waits:
                s = sems[w.sem] if isinstance(w.sem, str) else w.sem
                need[id(s)] = (s, max(w.value, need.get(id(s), (s, 0))[1]))
            for k, (s, v) in need.items():
                if known.get(k, 0) < v:
                    eng.wait_ge(s, v)
                    known[k] = v
            if fn is None:
                continue
            ins = fn(eng)
            if dsem is not None:
                ins.then_inc(dsem, 16)
            elif t.used:
                ins.then_inc(sems[e], 1)

    def number(self):
        for e, q in self.q.items():
            n = 0
            for fn, _, t, dsem in q:
                if dsem is None and t.used and fn is not None:
                    n += 1
                    t.value = n


class Slot:

    def __init__(self, ap):
        self.ap, self.free, self.held = ap, [], False


class Ring:
    def __init__(self, slots):
        self.slots, self.n = slots, 0

    def take(self):
        while self.slots[self.n % len(self.slots)].held:
            self.n += 1
        s = self.slots[self.n % len(self.slots)]
        self.n += 1
        return s


class Stream:

    def __init__(self, P, plan, stage, parts, sems):
        self.P, self.plan, self.stage, self.parts, self.sems = P, plan, stage, parts, sems
        self.loaded, self.prepared, self.got, self.released = 0, 0, 0, 0
        self.dma_tok, self.stage_free, self.split_tok = {}, {}, {}
        self.split_no = {}
        n = 0
        for i, (_, kind) in enumerate(plan):
            if kind == "split":
                self.split_no[i] = n
                n += 1
        self.part_free = {}
        self.pump()

    def pump(self):
        P = self.P
        moved = True
        while moved:
            moved = False
            i = self.loaded
            ns = len(self.stage)
            if i < len(self.plan) and (i < ns or i - ns in self.stage_free):
                t = P.dma("sp", self.sems[i % ns], self.stage[i % ns], self.plan[i][0],
                          self.stage_free.get(i - ns))
                self.dma_tok[i] = t
                self.loaded += 1
                moved = True
            i = self.prepared
            if i < self.loaded:
                if self.plan[i][1] != "split":
                    self.prepared += 1
                    moved = True
                else:
                    n = self.split_no[i]
                    np_ = len(self.parts)
                    if n < np_ or n - np_ in self.part_free:
                        hi, lo = self.parts[n % np_]
                        src = self.stage[i % ns]
                        th = P.op("act", lambda g, o=hi, s=src: g.activation(o, s, ACT.Copy),
                                  self.dma_tok[i], self.part_free.get(n - np_))
                        tl = P.op("dve", lambda g, o=lo, s=src, h=hi: g.tensor_tensor(o, s, h.bitcast(F32), ALU.subtract), th,
                                  self.dma_tok[i])
                        self.stage_free[i] = [tl, th]
                        self.split_tok[i] = [th, tl]
                        self.prepared += 1
                        moved = True

    def get(self):
        i = self.got
        self.got += 1
        if self.plan[i][1] == "split":
            return self.parts[self.split_no[i] % len(self.parts)], self.split_tok[i], i
        return self.stage[i % len(self.stage)], self.dma_tok[i], i

    def done(self, i, tok):
        if self.plan[i][1] == "split":
            self.part_free[self.split_no[i]] = [tok]
        else:
            self.stage_free[i] = [tok]
        self.pump()


def background():
    return [(name, g) for name, n in (("ada0", 12), ("ada1", 12), ("adb0", 6), ("adb1", 6)) for g in range(n)]


def unit_plan(A):
    plan = []

    def add(name, idx, kind="split"):
        plan.extend((A[name][i, :, :], kind) for i in idx)
    later = [(name, 4 * g + u) for name, g in background() for u in range(4)]

    def ada(n):
        for _ in range(n):
            if later:
                name, i = later.pop(0)
                add(name, [i])
    ada(16)
    for L in range(2):
        if L == 0:
            add("mgate", [0])
            for j in range(8):
                add("mqk", [j])
                ada(2)
            add("mv", range(8))
            for j in range(8):
                add("mo", [j])
                ada(2)
            add("mout", range(8))
        else:
            add("sqk", range(10))
            add("sv", range(2))
            add("sout", range(8))
        for g in range(4):
            for name in ("w1_", "w2_"):
                for k in range(8):
                    add(name + str(L), [8 * g + k])
                    ada(1)
    for L in range(2):
        add(f"p_gate{L}", [0])
        add(f"p_gqk{L}", range(4))
        add(f"p_gv{L}", range(4))
        for h in range(4):
            add(f"p_gg{L}", [h])
        for j in range(4):
            add(f"p_mg{L}", [2 * j, 2 * j + 1])
            add(f"br_g{L}", [j])
        add(f"p_aqk{L}", range(5))
        add(f"p_av{L}", [0])
        add(f"p_ag{L}", range(4))
        for j in range(4):
            add(f"p_ma{L}", [2 * j, 2 * j + 1])
            add(f"br_a{L}", [j])
        add(f"p_sv{L}", range(4))
        for h in range(4):
            add(f"p_su{L}", [h])
            add(f"p_sg{L}", [h])
        for j in range(4):
            add(f"p_ms{L}", [2 * j, 2 * j + 1])
            add(f"br_s{L}", [j])
        add(f"wo{L}", range(8))
    return plan


def trunk_kernel(nc, A, out, stop=None):
    ctx = ExitStack()
    with ctx:
        base = 16512
        at = [base]

        def place(name, shape, dt, offset=None):
            n = int(np.prod(shape[1:])) * (1 if dt == U8 else 4)
            if offset is None:
                offset = at[0]
                at[0] += (n + 31) // 32 * 32
            return nc.alloc_sbuf_tensor_at(name, shape, dt, offset=offset)

        NS, NR = 3, 4
        ctx.enter_context(nc.sbuf_tensor("fence", [128, (229344 - nc.sbuf_base) // 4 - 16], F32))
        stage = [place(f"stage{i}", [128, 1024], F32) for i in range(NS)]
        parts = [(place(f"whi{i}", [128, 1024], F32R), place(f"wlo{i}", [128, 1024], F32R)) for i in range(NR)]
        CM = place("CM", [128, 648], F32)
        CL = place("CL", [128, NCOLS], F32)
        CW = place("CW", [128, 32], F32)
        MODS = [place(f"MOD{i}", [128, 96], F32) for i in range(4)]
        C4 = [place(f"C4{i}", [128, 160], F32R) for i in range(2)]
        ROWS = place("ROWS", [4, 512], F32)
        MU = place("MU", [128, 96], F32)
        offH = at[0]
        Ht = place("Ht", [128, 8, TOK], F32)
        offU = at[0]
        U = place("U", [128, 2, 8, TOK], F32R)
        offY = at[0]
        Y = place("Y", [128, 2, 8, TOK], F32R)
        offZ = at[0]
        endZ = 229344
        HT = Ht[:, :, :]
        IDENT, ONES, BONES = CM[:, 0:128], CM[:, 128:256], CM[:, 256:384]
        SEL = CM[0:4, 640:642]
        BANDL, BANDR = CM[:, 384:512], CM[:, 512:640]

        PS = ctx.enter_context(nc.psum_tensor("PS", [128, 4096], F32))
        pairs = Ring([Slot(PS[:, 1024 * i:1024 * i + 1024]) for i in range(4)])

        sems = {e: ctx.enter_context(nc.semaphore(f"s_{e}")) for e in ("pe", "act", "dve", "pool", "sp")}
        wsem = [[ctx.enter_context(nc.semaphore(f"s_w{i}")), 0] for i in range(NS)]
        nsem = [0]

        def dsem():
            nsem[0] += 1
            return [ctx.enter_context(nc.semaphore(f"s_d{nsem[0]}")), 0]

        P = Prog()

        def act(o, i, f, *w, scale=1.0, bias=0.0, acc=None):
            return P.op("act", lambda g: g.activation(o, i, f, bias=bias, scale=scale, accum_out=acc), *w)

        def tt(o, a, b, op, *w, e="dve"):
            return P.op(e, lambda g: g.tensor_tensor(o, a, b, op), *w)

        def ts(o, a, s1, s2, op0, op1, *w, e="dve"):
            if op1 is None:
                return P.op(e, lambda g: g.tensor_scalar(o, a, s1, None, op0), *w)
            return P.op(e, lambda g: g.tensor_scalar(o, a, s1, s2, op0, op1), *w)

        def stt(o, a, s, b, op0, op1, *w):
            return P.op("dve", lambda g: g.scalar_tensor_tensor(o, a, s, b, op0, op1), *w)

        def copy(o, i, *w, e="dve"):
            return P.op(e, lambda g: g.tensor_copy(o, i), *w)

        def recip(o, i, *w):
            return P.op("dve", lambda g: g.reciprocal(o, i), *w)

        def scan(o, a, b, init, op0, op1, *w):
            return P.op("dve", lambda g: g.tensor_tensor_scan(o, a, b, init, op0, op1), *w)

        def mm(o, l, r, start, stop, *w):
            return P.op("pe", lambda g: g.matmul(o, l, r, start=start, stop=stop, skip_group_check=True), *w)

        def tr(o, i, k, *w):
            return P.op("pe", lambda g: g.transpose(o, i, IDENT[0:k, 0:k]), *w)

        def memset(o, v, *w, e="pool"):
            return P.op(e, lambda g: g.memset(o, v), *w)

        def split(hi, lo, src, *w):
            th = act(hi, src, ACT.Copy, *w)
            return [tt(lo, src, hi.bitcast(F32), ALU.subtract, th, *w), th]

        c1, c2 = dsem(), dsem()
        tc = [P.dma("sp", c1, CM[:, :], A["cmat"]), P.dma("sp", c2, CL[:, :], A["cols"])]
        hs = dsem()
        tH = P.dma("sp", hs, HT, A["hT"])
        W = Stream(P, unit_plan(A), [s[:, :] for s in stage], [(a[:, :], b[:, :]) for a, b in parts], wsem)
        t = memset(CW[:, 0:1], EPS)
        EPSC = CW[:, 0:1]
        te = [t, memset(CW[:, 1:2], 0.0)]
        P.op("act", lambda g: g.activation(CW[:, 2:3], EPSC, ACT.Copy), te, tc)
        P.op("dve", lambda g: g.tensor_copy(CW[:, 3:4], EPSC), te, tc)
        P.op("pe", None, tc)
        P.op("pool", None, tc)

        def col(name, i=0, n=1):
            a, _ = COLS[name]
            return CL[:, a + i:a + i + n]

        TG = ((0, 512), (512, 768))

        def xU(r, kt, a, b):
            return U[:, r, kt, a:b]

        def xY(r, kt, a, b):
            return Y[:, r, kt, a:b]

        def project(w, tw, x, nk, full, width=128, sub=0, mdim=128, waits=(), held=(), xt=None):
            s = pairs.take()
            wh, wl = (v.rearrange("p (k n) -> p k n", k=nk) for v in w)
            last = None
            if xt:
                for k in range(nk):
                    for a, b in (TG if full else TG[:1]):
                        for q, (xr, wv) in enumerate(((0, wh), (1, wh), (0, wl))):
                            last = mm(s.ap[0:mdim, a:b], wv[:, k, sub:sub + mdim], x(xr, k, a, b), k + q == 0,
                                      k == nk - 1 and q == 2, *([tw, s.free, waits] if k + q + a == 0 else []),
                                      *([xt[k]] if q + a == 0 else []))
                return s, last
            for a, b in (TG if full else TG[:1]):
                n = 0
                for (xr, wv) in ((0, wh), (1, wh), (0, wl)):
                    for k in range(nk):
                        last = mm(s.ap[0:mdim, a:b], wv[:, k, sub:sub + mdim], x(xr, k, a, b), n == 0,
                                  n == 3 * nk - 1, *([tw, s.free, waits] if n == 0 and a == 0 else []))
                        n += 1
            return s, last

        def projB(x, full=True, waits=(), held=(), xt=None):
            w, tw, i = W.get()
            s, last = project(w, tw, x, 8, full, 128, 0, 128, waits, held, xt)
            W.done(i, last)
            return s, last

        def projA(x, ntok, n, waits=()):
            nk = 1024 // n
            ss = [pairs.take() for _ in range((ntok + 1) // 2)]
            banks = [ss[t // 2].ap[:, 512 * (t % 2):512 * (t % 2) + n] for t in range(ntok)]
            for u in range(8 // nk):
                w, tw, i = W.get()
                wh, wl = (v.rearrange("p (k n) -> p k n", k=nk) for v in w)
                for t in range(ntok):
                    for kk in range(nk):
                        k = u * nk + kk
                        for q, (xr, wv) in enumerate(((0, wh), (1, wh), (0, wl))):
                            first = u == 0 and kk == 0 and q == 0
                            last = mm(banks[t], x(xr, k, 128 * t, 128 * t + 128), wv[:, kk, :], first,
                                      k == 7 and q == 2,
                                      *([tw, ss[t // 2].free, waits] if kk == 0 and q == 0 else []))
                W.done(i, last)
            return ss, banks, last

        SC = place("SC", [128, 32], F32, offZ)
        SCs = MU[:, 64:96]
        cc = COLS["cond"][0]
        t = act(SC[:, :], CL[:, cc:cc + 32], ACT.Exp, scale=-1.0)
        t = ts(SC[:, :], SC[:, :], 1.0, None, ALU.add, None, t)
        t = recip(SC[:, :], SC[:, :], t)
        tcond = tt(SCs, SC[:, :], CL[:, cc:cc + 32], ALU.mult, t)
        for b in range(2):
            t = P.op("act", lambda g, b=b: g.activation(C4[b][:, :], CM[:, 128:288], ACT.Copy, scale=0.0), tc)
            cv = C4[b][:, 0:32].rearrange("p (k v r) -> p k v r", v=2, r=2)
            sv = SCs[:, 16 * b:16 * b + 16].rearrange("p (k v) -> p k v", v=2)
            tcond = split(cv[:, :, :, 0], cv[:, :, :, 1], sv, tcond, t)

        later = background()
        todo = []
        rows_free = [None]
        tmod = [None]

        def ada_flush():
            if not todo:
                return
            t, dst, bias, g = todo.pop()
            s = pairs.take()
            for j in range(4):
                last = mm(s.ap[:, 2 * j:2 * j + 2], ROWS[0:4, 128 * j:128 * j + 128], SEL, True, True, t, s.free)
            rows_free[0] = [last]
            pv = s.ap[:, 0:8].rearrange("p (n v) -> p n v", v=2)
            dv = dst[:, 8 * g:8 * g + 8].rearrange("p (n v) -> p n v", v=2)
            s.free = [tt(dv[:, :, v], pv[:, :, v], bias[:, 4 * g:4 * g + 4], ALU.add, last) for v in range(2)]
            tmod[0] = s.free

        step = [0, None, None]

        def ada(n=4):
            for _ in range(n):
                if not later:
                    return
                u = step[0]
                if u == 0:
                    step[1] = pairs.take()
                    step[1].held = True
                s = step[1]
                name, g = later[0]
                b, L = int(name[2] == "b"), int(name[-1])
                w, tw, i = W.get()
                wh, wl = (v.rearrange("p (k n) -> p k n", k=2) for v in w)
                for kk in range(2):
                    k = 2 * u + kk
                    for wv in (wh, wl):
                        last = mm(s.ap[:, 0:512], C4[b][:, 4 * k:4 * k + 128], wv[:, kk, :], k == 0 and wv is wh,
                                  k == 7 and wv is wl, tw, s.free if k == 0 else None, tcond if k == 0 else None)
                W.done(i, last)
                if u == 1:
                    ada_flush()
                step[0] = (u + 1) % 4
                if u == 3:
                    bias = col(("ada2_b" if b else "ada_b") + str(L), 0, 24 if b else 48)
                    t = act(ROWS[0:4, :], s.ap[0:4, 0:512], ACT.Copy, last, rows_free[0])
                    s.free = [t]
                    s.held = False
                    todo.append((t, MODS[2 * b + L], bias, g))
                    later.pop(0)

        cur = [0]

        def mod(i, kt, v):
            return MODS[cur[0]][:, 2 * (8 * i + kt) + v:2 * (8 * i + kt) + v + 1]

        def modall(i, v):
            return MODS[cur[0]][:, 16 * i:16 * i + 16].rearrange("p (k v) -> p k v", v=2)[:, :, v]

        def groups(full):
            return ((0, LAT, 0), (LAT, TOK, 1)) if full else ((0, LAT, 0),)

        ACC = place("ACC", [128, TOK], F32, offZ + 24576)
        SQ = Ring([Slot(place(f"SQ{i}", [128, TOK], F32, offZ + 27648 + 3072 * i)[:, :]) for i in range(2)])
        acc = [None]

        def square_in(k, N, w):
            if k == 0:
                acc[0] = act(ACC[:, 0:N], HT[:, k, 0:N], ACT.Square, w)
            else:
                q = SQ.take()
                t = act(q.ap[:, 0:N], HT[:, k, 0:N], ACT.Square, w, q.free)
                if k == 7:
                    acc.append((q, t))
                    return
                acc[0] = tt(ACC[:, 0:N], ACC[:, 0:N], q.ap[:, 0:N], ALU.add, t, acc[0], e="pool")
                q.free = [acc[0]]

        ROOTS = Ring([Slot(MU[:, 32 + 16 * i:48 + 16 * i]) for i in range(4)])
        for rs_ in ROOTS.slots:
            rs_.free = [tcond]

        def inverse_root(srcs, n, scale, take=None):
            s = take() if take else pairs.take()
            r = ROOTS.take()
            for i, (x, tx) in enumerate(srcs):
                for c in range(n):
                    o = s.ap[:, 896 + c:897 + c]
                    last = mm(o, x[:, 128 * c:128 * c + 128], ONES[:, 0:1], i == 0 and c == 0, i == len(srcs) - 1, tx, s.free)
            read = last
            t = act(r.ap[:, 0:n], s.ap[:, 896:896 + n], ACT.Sqrt, last, r.free, scale=scale, bias=EPSC)
            t = recip(r.ap[:, 0:n], r.ap[:, 0:n], t)
            for c in range(n):
                last = mm(s.ap[:, 128 * c:128 * c + 128], r.ap[:, c:c + 1].to_broadcast([128, 128]), IDENT, c % 4 == 0, True, t)
            r.free = [last]
            return s, last, read

        def root(full):
            q, tq = acc.pop()
            s, last, read = inverse_root([(ACC, acc[0]), (q.ap, tq)], 6 if full else 4, 1.0 / D)
            q.free = [read]
            return s, last

        def norm_mod(L, gain, ish, full, dst):
            T1 = Ring([Slot(place(f"nt{L}{ish}{i}", [128, TOK], F32, offZ + 9216 + 3072 * i)[:, :]) for i in range(4)])
            tg = None
            for v in range(2):
                t = ts(MU[:, 8 * v:8 * v + 8], modall(ish + 1, v), 1.0, None, ALU.add, None, tmod[0])
                tg = tt(MU[:, 8 * v:8 * v + 8], MU[:, 8 * v:8 * v + 8], gain, ALU.mult, t)
            sr, tr_ = root(full)
            N = TOK if full else LAT
            ready = []
            prev, prev2 = None, None
            for k in range(10):
                if k < 8:
                    a = T1.take()
                    t = tt(a.ap[:, 0:N], HT[:, k, 0:N], sr.ap[:, 0:N], ALU.mult, tr_, a.free)
                    sr.free = [t]
                    tl = [act(a.ap[:, lo:hi_], a.ap[:, lo:hi_], ACT.Identity, t, tg,
                              scale=MU[:, 8 * v + k:8 * v + k + 1], bias=mod(ish, k, v)) for lo, hi_, v in groups(full)]
                th = None
                if prev is not None:
                    th = act(dst[:, 0, k - 1, 0:N], prev[0].ap[:, 0:N], ACT.Copy, prev[1])
                if prev2 is not None:
                    pa, ptl, ph = prev2
                    pa.free = [ph, tt(dst[:, 1, k - 2, 0:N], pa.ap[:, 0:N], dst[:, 0, k - 2, 0:N].bitcast(F32),
                                      ALU.subtract, ptl, ph)]
                    ready.append(pa.free)
                prev2 = (*prev, th) if prev is not None else None
                prev = (a, tl) if k < 8 else None
            P.barrier(free=("pe",))
            return ready

        def residual(gidx, s, k, last, full, final):
            for lo, hi_, v in groups(full):
                t = stt(HT[:, k, lo:hi_], s.ap[:, lo:hi_], mod(gidx, k, v), HT[:, k, lo:hi_], ALU.mult, ALU.add, last)
            s.free = [t]
            if final:
                square_in(k, TOK if full else LAT, t)
            return t

        def out_proj(x, gidx, full, xt):
            for k in range(8):
                s, last = projB(x, full, xt=xt if k == 0 else None)
                residual(gidx, s, k, last, full, True)
            P.barrier()

        def ffn(L, full):
            N = TOK if full else LAT
            ready = norm_mod(L, col(f"norm_ffn{L}", 0, 8), 3, full, U)
            T = Ring([Slot(place(f"ff{L}{i}", [128, TOK], F32, offZ + 3072 * i)[:, :]) for i in range(3)])
            T2 = Ring([Slot(place(f"fg{L}{i}", [128, TOK], F32, offZ + 9216 + 3072 * i)[:, :]) for i in range(3)])
            yfree = None
            for g in range(4):
                ty = []
                for k in range(8):
                    s, last = projB(xU, full, xt=ready if g == 0 else None)
                    a, b = T.take(), T2.take()
                    t = act(a.ap[:, 0:N], s.ap[:, 0:N], ACT.Relu, last, a.free)
                    s.free = [t]
                    t = tt(b.ap[:, 0:N], a.ap[:, 0:N], a.ap[:, 0:N], ALU.mult, t, b.free)
                    a.free = [t]
                    b.free = split(Y[:, 0, k, 0:N], Y[:, 1, k, 0:N], b.ap[:, 0:N], t, yfree)
                    ty.append(b.free)
                    ada(1)
                for k in range(8):
                    w, tw, i = W.get()
                    s, last = project(w, tw, xY, 8, full, xt=ty)
                    W.done(i, last)
                    residual(5, s, k, last, full, g == 3)
                    yfree = last
                    ada(1)
            ada_flush()
            P.barrier()

        def attention(tag, nh, nkv, qt, kt, V, tiles, ytile, offs, sink=None):
            group = nh // nkv
            o = offs
            ng = nh // 8
            Pr = Ring([Slot(place(f"P{tag}{i}", [128, 768], F32, o + 3072 * i)[:, :]) for i in range(3)])
            PTr = Ring([Slot(place(f"PT{tag}{i}", [128, 768], F32, o + 9216 + 3072 * i)[:, :]) for i in range(2)])
            STr = Ring([Slot(place(f"ST{tag}{i}", [128, 4], F32, o + 15360 + 32 * i)) for i in range(4)])
            prs = pairs.slots
            Sr = Ring([prs[0], prs[1]])
            Tp = prs[2]
            Ob = Ring([Slot(prs[3].ap[:, 512 * i:512 * i + 512]) for i in range(2)])
            for s in Ob.slots:
                s.free = list(prs[3].free)
            jobs = [(ti, gi, h) for ti in range(len(tiles)) for gi in range(ng) for h in range(8)]
            state = {}

            def scores(n):
                ti, gi, i = jobs[n]
                q0, keys = tiles[ti]
                h = 8 * gi + i
                g = h // group
                st = STr.take()
                s = Sr.take()
                qv = qt(h, q0)
                c = 0
                for (k0, kn, mask) in keys:
                    while kn > 0:
                        m = min(kn, 512 - c % 512)
                        last = mm(s.ap[:, c:c + m], qv, kt(g, k0, m), c % 512 == 0, True, s.free)
                        if mask is not None:
                            last = mm(s.ap[:, c:c + m], IDENT, mask, False, True)
                        c, k0, kn = c + m, k0 + m, kn - m
                mx, nm, sm, rd = (st.ap[:, j:j + 1] for j in range(4))
                t = P.op("dve", lambda g_: g_.tensor_reduce(mx, s.ap[:, 0:c], AX.X, ALU.max), last, st.free)
                if sink is not None:
                    t = ts(nm, mx, -0.125, sink[:, h:h + 1], ALU.mult, ALU.min, t)
                else:
                    t = ts(nm, mx, -0.125, None, ALU.mult, None, t)
                p = Pr.take()
                t = act(p.ap[:, 0:c], s.ap[:, 0:c], ACT.Exp, t, p.free, scale=0.125, bias=nm, acc=sm)
                s.free = [t]
                if sink is not None:
                    t = [t, act(mx, sink[:, h:h + 1], ACT.Exp, t, scale=-1.0, bias=nm)]
                state[n] = (h, st, p, c, t)

            def divide(n):
                h, st, p, c, t = state[n]
                mx, nm, sm, rd = (st.ap[:, j:j + 1] for j in range(4))
                if sink is not None:
                    t = tt(sm, sm, mx, ALU.add, t)
                t = recip(rd, sm, t)
                t = ts(p.ap[:, 0:c], p.ap[:, 0:c], rd, None, ALU.mult, None, t)
                st.free = [t]
                state[n] = (p, c, t)

            def turn(n):
                p, c, t = state[n]
                for b in range(c // 128):
                    last = tr(Tp.ap[:, 128 * b:128 * b + 128], p.ap[:, 128 * b:128 * b + 128], 128, t, Tp.free)
                p.free = [last]
                pt = PTr.take()
                ca = min(c, 512)
                w = [copy(pt.ap[:, 0:ca], Tp.ap[:, 0:ca], last, pt.free)]
                if c > ca:
                    w.append(act(pt.ap[:, ca:c], Tp.ap[:, ca:c], ACT.Copy, last, pt.free))
                Tp.free = w
                state[n] = (pt, w)

            def values(n):
                ti, gi, i = jobs[n]
                q0, keys = tiles[ti]
                g = (8 * gi + i) // group
                pt, w = state.pop(n)
                if i == 0:
                    state["o"] = Ob.take()
                ob = state["o"]
                rows = slice(64 * (i % 2), 64 * (i % 2) + 64)
                blocks = [k0 + 128 * b for (k0, kn, _) in keys for b in range(kn // 128)]
                for b, k0 in enumerate(blocks):
                    last = mm(ob.ap[rows, 128 * (i // 2):128 * (i // 2) + 128], V(k0 // 128, g),
                              pt.ap[:, 128 * b:128 * b + 128], b == 0, b == len(blocks) - 1, w, ob.free)
                pt.free = [last]
                if i == 7:
                    ob.free = ytile(q0, 4 * gi, ob.ap.rearrange("p (f t) -> p f t", t=128), last)

            N = len(jobs)
            for n in range(N + 4):
                if n < N:
                    scores(n)
                if 0 <= n - 1 < N:
                    divide(n - 1)
                if 0 <= n - 2 < N:
                    turn(n - 2)
                if 0 <= n - 3 < N:
                    values(n - 3)
            prs[3].free = [x for s in Ob.slots for x in s.free]
            pairs.n = 0

        def odd_half(x, y, *w):
            t0 = memset(y[0:64, :], 0.0, *w)
            t = copy(y[64:128, :], x[64:128, :], *w)
            return [t0, t, memset(x[64:128, :], 0.0, t, e="dve")]

        def rope(x, CS, tile_tok, scr, w):
            s = pairs.take()
            last = mm(s.ap[:, 0:512], tile_tok, x, True, True, w, s.free)
            a = scr.take()
            t1 = tt(a.ap[:, 0:512], s.ap[:, 0:512], CS[:, 1, :], ALU.mult, last, a.free)
            s.free = [t1]
            t2 = tt(x, x, CS[:, 0, :], ALU.mult, last, t1)
            t = tt(x, x, a.ap[:, 0:512], ALU.add, t1, t2)
            a.free = [t]
            return t

        def take_not(*held):
            s = pairs.take()
            while s in held:
                s = pairs.take()
            return s

        def log_sigmoid(z, tmp, w):
            t = stt(tmp, z, -1.0, z, ALU.mult, ALU.max, w)
            t = act(tmp, tmp, ACT.Exp, t, scale=-1.0)
            t = ts(tmp, tmp, 1.0, None, ALU.add, None, t)
            t = act(tmp, tmp, ACT.Ln, t)
            return stt(z, z, 0.0, tmp, ALU.min, ALU.subtract, t)

        def mlstm(ready):
            QK = place("mQK", [128, 8, TOK], F32, offY)
            OT = place("mO", [128, 8, TOK], F32, offY + 24576)
            V = place("mV", [128, 6, 8, 129], F32, offZ)
            IR = place("mI", [128, TOK], F32, offZ + 24768)
            FZ = place("mFz", [128, TOK], F32, offZ + 27840)
            aT = place("maT", [128, 6, 40], F32, offZ + 30912)
            eT = place("meT", [128, 6, 40], F32, offZ + 31872)
            ZR = place("mZR", [128, 512], F32, offZ + 32832)
            tv1 = memset(V[:, :, :, 128], 1.0)
            tz = memset(ZR[0:1, :], 0.0)
            s, last = projB(xU, xt=ready)
            t1 = copy(IR[0:40, :], s.ap[0:40, 0:TOK], last)
            t2 = copy(FZ[0:40, :], s.ap[64:104, 0:TOK], last)
            s.free = [t1, t2]
            ti = ts(IR[0:40, :], IR[0:40, :], col("gb_i")[0:40], None, ALU.add, None, t1)
            tf = ts(FZ[0:40, :], FZ[0:40, :], col("gb_f")[0:40], None, ALU.add, None, t2)
            F_ = place("mF", [128, TOK], F32, offY + 24576)
            TM = place("mTM", [128, TOK], F32, offY + 27648)
            AR = place("mA", [128, TOK], F32, offY + 30720)
            MR = place("mM", [128, TOK], F32, offZ + 27840)
            MM = place("mMM", [128, TOK], F32, offY + 33792)
            r = slice(0, 40)
            t = log_sigmoid(FZ[r, :], TM[r, :], tf)
            t0 = memset(F_[r, :], 0.0, e="dve")

            def both(dst, src, op, w):
                out_ = []
                for rows, rev in ((slice(0, 8), False), (slice(32, 40), True)):
                    def v(x, a, b):
                        y = x[rows, a:b]
                        return y[:, ::-1] if rev else y
                    t = scan(v(dst, 512, 768), v(src, 512, 768), v(src, 512, 768), 0.0, op, ALU.bypass, w)
                    init = dst[rows, 512:513] if rev else dst[rows, 767:768]
                    out_.append(scan(v(dst, 0, 512), v(src, 0, 512), v(src, 0, 512), init, op, ALU.bypass, t))
                return out_
            t = both(F_, FZ, ALU.add, [t, t0])
            t = tt(AR[r, :], IR[r, :], F_[r, :], ALU.subtract, t, ti)
            ta = t
            t0 = memset(MR[r, :], 0.0, t, e="dve")
            t = both(MR, AR, ALU.max, [t, t0])
            tm_ = t
            t = tt(MM[r, :], F_[r, :], MR[r, :], ALU.add, t)
            tmm = t

            for j in range(8):
                s, last = projB(xU)
                s.free = [act(QK[:, j, :], s.ap[:, 0:TOK], ACT.Copy, last, scale=1.0 if j < 4 else 0.125)]
                ada(2)
            s = pairs.take()
            for i in range(6):
                l1 = tr(s.ap[:, 40 * i:40 * i + 40], AR[r, 128 * i:128 * i + 128], 40, ta, s.free)
            for i in range(6):
                l2 = tr(s.ap[:, 512 + 40 * i:552 + 40 * i], MM[r, 128 * i:128 * i + 128], 40, tmm)
            t1 = copy(aT[:, :, :], s.ap[:, 0:240].rearrange("p (i r) -> p i r", r=40), l1)
            t2 = act(eT[:, :, :], s.ap[:, 512:752].rearrange("p (i r) -> p i r", r=40), ACT.Exp, l2, scale=-1.0)
            s.free = [t1, t2]
            gates_read = [l1, l2]
            for g in range(2):
                ss, banks, last = projA(xU, 6, 512)
                for i in range(6):
                    o = V[:, i, 4 * g:4 * g + 4, 0:128]
                    src = banks[i].rearrange("p (h e) -> p h e", e=128)
                    t = (copy(o, src, last) if i % 2 else act(o, src, ACT.Copy, last))
                    ss[i // 2].free = (ss[i // 2].free if i % 2 else []) + [t]
            for j in range(8):
                s, last = projB(xU)
                s.free = [act(OT[:, j, :], s.ap[:, 0:TOK], ACT.Sigmoid, last, gates_read)]
                ada(2)
            ada_flush()
            P.barrier(free=("pe",))
            MB = [[place(f"mMB{i}{d}", [128, TOK], F32, offU + 12288 + 3072 * (2 * i + d)) for d in range(2)]
                  for i in range(2)]
            ER = Ring([Slot(place(f"mE{i}", [128, TOK], F32, o)[:, :])
                       for i, o in enumerate((offU + 24576, offU + 27648, offZ + 24768, offU + 9216))])
            DG = [[Slot(place(f"mDG{i}{d}", [128, TOK], F32, offU + 30720 + 3072 * (2 * i + d))[:, :]) for d in range(2)]
                  for i in range(2)]
            HA = place("mHA", [128, 6, 128], F32, offU + 43008)
            HB = place("mHB", [128, 6, 128], F32, offU + 46080)
            DN = place("mDN", [128, 4, 6], F32, offZ + 34880)
            KZ = [place(f"mKZ{i}", [128, TOK], F32, offU + 3072 * i) for i in range(2)]
            tkz = [memset(KZ[0][64:128, :], 0.0, e="dve"), memset(KZ[1][0:64, :], 0.0, e="dve")]
            kzfree = [None, None]
            mbfree = [None, None]
            thead = [None]
            prep, hold = {}, []

            def head_start(h):
                pb = 64 * (h % 2)
                kz = KZ[h % 2]
                tk = copy(kz[pb:pb + 64, :], QK[pb:pb + 64, 4 + h // 2, :], kzfree[h % 2], e="pool")
                tmb, tdg = [], []
                for d in range(2):
                    s = take_not(*hold)
                    row = 32 * d + h
                    for a, b in TG:
                        last = mm(s.ap[:, a:b], IDENT[0:40, row:row + 1].to_broadcast([40, 128]), MR[r, a:b], True, True,
                                  s.free)
                    t = act(MB[h % 2][d][:, :], s.ap[:, 0:TOK], ACT.Copy, last, mbfree[h % 2])
                    s.free = [t]
                    tmb.append(t)
                    dgs = DG[h % 2][d]
                    dv = dgs.ap.rearrange("p (c e) -> p c e", e=128)
                    t = tt(dv, MB[h % 2][d][:, :].rearrange("p (c e) -> p c e", e=128),
                           aT[:, :, row:row + 1].to_broadcast([128, 6, 128]), ALU.subtract, t, dgs.free)
                    t = ts(dgs.ap, dgs.ap, 0.0, None, ALU.max, None, t)
                    t = act(dgs.ap, dgs.ap, ACT.Exp, t, scale=-1.0)
                    sg = 1 if d == 0 else -1
                    tdg.append(P.op("pool", lambda g, dv=dv, sg=sg: g.affine_select(
                        out=dv, in_=dv, compare_op=ALU.is_ge, fill=0.0, base=0, pattern=[[0, 6], [sg, 128]],
                        channel_multiplier=-sg), t))
                prep[h] = (kz, tk, tmb, tdg)

            def block_scores(h, i):
                kz, tk, tmb, tdg = prep[h]
                s = take_not(*hold)
                for a, b in (TG if i >= 4 else TG[:1]):
                    last = mm(s.ap[:, a:b], kz[:, 128 * i:128 * i + 128], QK[:, h // 2, a:b], True, True, s.free, tk, tkz)
                kzfree[h % 2] = [last]
                work, sfree = [], []
                for d in range(2):
                    row = 32 * d + h
                    if d == 0:
                        rg = [(128 * i + 128, 512)] if i < 3 else [[], [(0, 512), (640, 768)], [(0, 512)]][i - 3]
                    else:
                        rg = [(0, 128 * i)] if i > 0 else []
                    dgs = DG[h % 2][d]
                    dg = dgs.ap[:, 128 * i:128 * i + 128]
                    td = tt(dg, dg, s.ap[:, 128 * i:128 * i + 128], ALU.mult, last, tdg[d])
                    sfree.append(td)
                    work.append((d, dgs, [(dg, i)], td))
                    if rg:
                        e = ER.take()
                        te_ = [act(e.ap[:, a:b], MB[h % 2][d][:, a:b], ACT.Exp, tmb[d], e.free, scale=-1.0,
                                   bias=aT[:, i, row:row + 1]) for a, b in rg]
                        mbfree[h % 2] = te_
                        tw = [tt(e.ap[:, a:b], e.ap[:, a:b], s.ap[:, a:b], ALU.mult, last, te_) for a, b in rg]
                        sfree += tw
                        work.append((d, e, [(e.ap[:, 128 * q:128 * q + 128], q) for a, b in rg
                                            for q in range(a // 128, b // 128)], tw))
                s.free = sfree
                return work

            def block_values(h, i, work):
                for d, slot, tiles_, tw in work:
                    for l_, q in tiles_:
                        cc_ = 512 * (q // 3) + 129 * (q % 3)
                        lo_ = mm(hold[d].ap[:, cc_:cc_ + 129], l_, V[:, i, h, :], False, False, tw, tv1)
                    slot.free = [lo_]
                return lo_

            def normalise(h, lo_):
                view = [o.ap.rearrange("p (b c) -> p b c", c=512)[:, :, 0:387].rearrange("p b (t e) -> p b t e", e=129)
                        for o in hold]
                tn = []
                for d, dst in ((0, HA), (1, HB)):
                    dv = DN[:, d, :].rearrange("p (b t) -> p b t", t=3)
                    t = act(dv, view[d][:, :, :, 128], ACT.Abs, lo_, thead[0])
                    t = tt(DN[:, d, :], DN[:, d, :], eT[:, :, 32 * d + h], ALU.max, t)
                    t = recip(DN[:, d, :], DN[:, d, :], t)
                    hold[d].free = [tt(dst[:, 3 * b:3 * b + 3, :], view[d][:, b, :, 0:128],
                                       DN[:, d, 3 * b:3 * b + 3].unsqueeze(2).to_broadcast([128, 3, 128]), ALU.mult,
                                       t, thead[0]) for b in range(2)]
                    tn += hold[d].free
                return tn

            def head_norm(tn):
                t = tt(HA[:, :, :], HA[:, :, :], HB[:, :, :], ALU.add, tn)
                t = tt(HB[:, :, :], HA[:, :, :], HA[:, :, :], ALU.mult, t)
                t = P.op("dve", lambda g: g.tensor_reduce(DN[:, 2, :], HB[:, :, :], AX.X, ALU.add), t)
                t = act(DN[:, 3, :], DN[:, 2, :], ACT.Sqrt, t, scale=1.0 / 128, bias=EPSC)
                t = recip(DN[:, 3, :], DN[:, 3, :], t)
                return tt(HA[:, :, :], HA[:, :, :], DN[:, 3, :].unsqueeze(2).to_broadcast([128, 6, 128]), ALU.mult, t)

            def head_out(h, t):
                s = take_not(*hold)
                for i in range(6):
                    last = tr(s.ap[:, 128 * i:128 * i + 128], HA[:, i, :], 128, t, s.free)
                thead[0] = last
                s.free = [stt(OT[:, h, :], s.ap[:, 0:TOK], col("head_norm", h), OT[:, h, :], ALU.mult, ALU.mult, last)]

            head_start(0)
            tail = None
            for h in range(8):
                hold[:] = [pairs.take(), pairs.take()]
                for o in hold:
                    for b in range(2):
                        mm(o.ap[:, 512 * b:512 * b + 387], ZR[0:1, 0:128], ZR[0:1, 0:387], True, False, o.free, tz)
                before = block_scores(h, 0)
                for i in range(6):
                    work = before
                    if i < 5:
                        before = block_scores(h, i + 1)
                    if i == 0 and tail is not None:
                        tail = head_norm(tail)
                    if i == 2 and tail is not None:
                        head_out(h - 1, tail)
                    if i == 3 and h < 7:
                        head_start(h + 1)
                    lo_ = block_values(h, i, work)
                tail = normalise(h, lo_)
            hold[:] = []
            head_out(7, head_norm(tail))
            P.barrier(free=("pe",))
            tu = [split(U[:, 0, h, :], U[:, 1, h, :], OT[:, h, :]) for h in range(8)]
            out_proj(xU, 2, True, tu)

        def swa(ready):
            Q = place("sQ", [128, 8, 512], F32, offZ)
            K = place("sK", [128, 2, TOK], F32, offZ + 16384)
            V = place("sV", [128, 6, 256], F32, offZ + 22528)
            CS = place("sCS", [128, 2, 512], F32, offZ + 28672)
            RM = place("sRM", [128, 128], F32, offZ + 32768)
            NSK = place("sNS", [128, 16], F32, offZ + 33280)
            d1, d2 = dsem(), dsem()
            tcs = [P.dma("sp", d1, CS[:, :, :], A["rope_s"], P.newest["dve"]),
                   P.dma("sp", d2, RM[:, :], A["rot_s"])]
            scr = Ring([Slot(place(f"sr{i}", [128, 512], F32, offY + 2048 * i)[:, :]) for i in range(2)])
            turned = []
            for j in range(11):
                if j < 10:
                    s, last = projB(xU, j >= 8, xt=ready if j in (0, 8) else None)
                if j < 8:
                    s.free = [act(Q[:, j, :], s.ap[:, 0:512], ACT.Copy, last)]
                elif j < 10:
                    s.free = [act(K[:, j - 8, :], s.ap[:, 0:TOK], ACT.Copy, last)]
                if j > 0:
                    turned.append(rope(Q[:, j - 1, :] if j < 9 else K[:, j - 9, 0:512], CS, RM[:, :], scr,
                                       [tcs, before]))
                before = s.free
            ss, banks, last = projA(xU, 6, 256)
            for i in range(6):
                t = copy(V[:, i, :], banks[i], last)
                ss[i // 2].free = [t]
            tn = ts(NSK[:, :], col("sink", 0, 16), -1.0, None, ALU.mult, None)
            P.barrier(free=("pe",))

            def place_of(h):
                g = h // 4
                return 4 * (g // 2) + h % 4, 64 * (g % 2)

            KO = place("sKO", [128, 2, TOK], F32, offU + 16384)
            tko = [odd_half(K[:, j, :], KO[:, j, :], turned) for j in range(2)]

            def qt(h, q0):
                return Q[:, place_of(h)[0], q0:q0 + 128]

            def kt(g, k0, m):
                return (KO if g % 2 else K)[:, g // 2, k0:k0 + m]

            tiles = []
            for j in range(4):
                keys = []
                if j > 0:
                    keys.append((128 * (j - 1), 128, BANDL))
                keys.append((128 * j, 128, None))
                if j < 3:
                    keys.append((128 * (j + 1), 128, BANDR))
                keys.append((512, 256, None))
                tiles.append((128 * j, keys))

            def ytile(q0, f, ap, last):
                hi, lo = Y[:, 0, f:f + 4, q0:q0 + 128], Y[:, 1, f:f + 4, q0:q0 + 128]
                ytok.append(split(hi, lo, ap, last))
                return ytok[-1]
            ytok = []
            P.op("pe", None, tko, turned, tn, before)
            attention("s", 16, 4, qt, kt, lambda b, g: V[:, b, 64 * g:64 * g + 64], tiles, ytile, offU, NSK[:, :])
            P.barrier(free=("pe",))
            out_proj(xY, 2, False, [ytok] * 8)

        for k in range(8):
            square_in(k, TOK, tH)
        for _ in range(4):
            ada()
            ada_flush()
        for L in range(2):
            full = L == 0
            cur[0] = L
            ready = norm_mod(L, col(f"norm_mix{L}", 0, 8), 0, True, U)
            if L == 0:
                mlstm(ready)
            else:
                swa(ready)
            if stop == f"mix{L}":
                break
            if L == 1 and (stop is None or stop.startswith("b")):
                tctx = P.dma("sp", dsem(), HT[:, :, 512:768], A["ctx2T"],
                             [t for t in P.newest.values() if t.sem != "sp"])
            ffn(L, full)
            if stop == f"l{L}":
                break

        XS = nc.dram_tensor("XS", (128, 8, TOK), F32, kind="Internal").ap()
        offY2 = offY + 24576
        Y4 = place("Y4", [128, 2, 4, TOK], F32R, offY)

        def xY4(r, kt, a, b):
            return Y4[:, r, kt, a:b]

        def split_into(dst, k, src, N, w):
            return split(dst[:, 0, k, 0:N], dst[:, 1, k, 0:N], src, w)

        def merge(first, full, tag, ytok, sfree):
            N = TOK if full else LAT
            SG = Ring([Slot(place(f"mg{tag}{i}", [128, TOK], F32, offZ + 3072 * i)[:, :]) for i in range(3)])
            for g in SG.slots:
                g.free = sfree
            for j4 in range(4):
                gates = [projB(xU, full) for _ in range(2)]
                wb, twb, ib = W.get()
                sg = []
                for s1, last1 in gates:
                    g = SG.take()
                    t = act(g.ap[:, 0:N], s1.ap[:, 0:N], ACT.Sigmoid, last1, g.free)
                    s1.free = [t]
                    sg.append((g, t))
                for jj in range(2):
                    j = 2 * j4 + jj
                    s2, last2 = project(wb, twb, xY4, 4, full, 256, 128 * jj, xt=ytok if j == 0 else None)
                    g, t = sg[jj]
                    if first:
                        t = tt(HT[:, j, 0:N], g.ap[:, 0:N], s2.ap[:, 0:N], ALU.mult, t, last2)
                        s2.free = g.free = [t]
                    else:
                        t = tt(g.ap[:, 0:N], g.ap[:, 0:N], s2.ap[:, 0:N], ALU.mult, t, last2)
                        s2.free = [t]
                        g.free = [tt(HT[:, j, 0:N], HT[:, j, 0:N], g.ap[:, 0:N], ALU.add, t)]
                W.done(ib, last2)
            P.barrier(free=("pe",))

        def gla(L, full, ready):
            n = f"g{L}"
            B_ = place(n + "b", [128, 4, TOK], F32, offY2)
            QK = place(n + "qk", [128, 4, TOK], F32, offY2 + 12288)
            V = place(n + "v", [128, 6, 512], F32, offZ)
            S = place(n + "s", [128, 4, 6, 128], F32, offZ + 12288)
            QB = place(n + "qb", [128, 2, TOK], F32, offZ + 24576)
            T0 = place(n + "t0", [128, TOK], F32, offZ + 30720)
            A2 = place(n + "a2", [128, 256], F32, offZ + 33792)
            DEC = place(n + "dec", [128, 4, 6], F32, offZ + 34816)
            ATT = [place(n + f"att{i}", [128, TOK], F32, offH + 3072 * i) for i in range(2)]
            MKW = place(n + "mk", [128, 14, 96], I32, offH + 6144)
            MK = MKW[:, :, :].bitcast(U8)
            RES = place(n + "res", [128, 2, TOK], F32, offZ + 12288)
            AF = place(n + "af", [128, TOK], F32, offZ + 24576)
            T1 = place(n + "t1", [128, TOK], F32, offH + 20736)
            T2 = place(n + "t2", [128, TOK], F32, offY + 6144)
            TR = Ring([Slot(T0[:, :]), Slot(T1[:, :]), Slot(T2[:, :])])
            TR.slots[1].free = [tXS]
            NC_ = 6 if full else 4
            w0 = [t for t in P.newest.values() if t.sem != "sp"]
            d = [dsem() for _ in range(3)]
            ta2 = P.dma("sp", d[2], A2[0:64, :], A[f"a2_{L}"], w0)
            trs = P.dma("sp", d[1], RES[:, :, :], A["reset"])
            tmk = P.dma("sp", d[0], MKW[:, :, :], A["gmask"], tXS)
            ZKT = [place(n + f"zk{i}", [128, TOK], F32, (offH + 11520 + 3072 * i) if i < 3 else offY + 9216)
                   for i in range(4)]
            ZK = Ring([Slot([ZKT[2 * i], ZKT[2 * i + 1]]) for i in range(2)])
            tzk = [memset(z[:, :], 0.0, w0, tXS) for z in ZKT]
            s, last = projB(xU, xt=ready)
            taf = act(AF[0:64, :], s.ap[0:64, 0:TOK], ACT.Copy, last)
            s.free = [taf]
            tb_, tqk = [None] * 4, [None] * 4

            def gate(m):
                d_, f = m // 2, m % 2
                s = pairs.take()
                for a, b in TG:
                    last = mm(s.ap[:, a:b], A2[32 * d_:32 * d_ + 16, 128 * f:128 * f + 128],
                              AF[32 * d_:32 * d_ + 16, a:b], True, True, taf, ta2, s.free)
                z = B_[:, m, :]
                t = act(z, s.ap[:, 0:TOK], ACT.Identity, last, bias=col(("abf" if d_ == 0 else "abb") + str(L), f))
                s.free = [t]
                x = TR.take()
                t = log_sigmoid(z, x.ap, [t, x.free])
                x.free = [t]
                t = ts(z, z, 1.0 / 16, None, ALU.mult, None, t)
                rv, zv = RES[:, d_, :], z
                if d_:
                    rv, zv = rv[:, ::-1], zv[:, ::-1]
                tb_[m] = scan(zv, rv, zv, 0.0, ALU.mult, ALU.add, t, trs)
                return last

            for j in range(4):
                s, last = projB(xU)
                s.free = [act(QK[:, j, :], s.ap[:, 0:TOK], ACT.Copy, last, scale=0.125 if j < 2 else 1.0)]
                tqk[j] = s.free
                tgl = gate(j)
            KD = [T0[:, :], T1[:, :], QB[:, 0, :], QB[:, 1, :]]
            tkd, tdec = [], []
            for m in range(4):
                d_, f = m // 2, m % 2
                end = 127 if d_ == 0 else 0
                bv = B_[:, m, :].rearrange("p (c e) -> p c e", e=128)
                tdec.append(act(DEC[:, m, :], bv[:, :, end], ACT.Exp, tb_[m]))
                xv = KD[m].rearrange("p (c e) -> p c e", e=128)
                t = tt(xv, bv[:, :, end:end + 1].to_broadcast([128, 6, 128]), bv, ALU.subtract, tb_[m], tgl,
                       [x.free for x in TR.slots])
                t = act(KD[m], KD[m], ACT.Exp, t)
                tkd.append(tt(KD[m], KD[m], QK[:, 2 + f, :], ALU.mult, t, tqk[2 + f]))
            ss, banks, last = projA(xU, 6, 512)
            tv = []
            for i in range(6):
                if i % 2:
                    tv.append(act(V[:, i, :], banks[i], ACT.Copy, last))
                    ss[i // 2].free = tv[-2:]
                else:
                    tv.append(copy(V[:, i, :], banks[i], last))

            tS = []
            ktfree = [tXS, tXS]
            turned = []
            for m in range(5):
                if m < 4:
                    s = pairs.take()
                    for c in range(6):
                        last = tr(s.ap[:, 128 * c:128 * c + 128], KD[m][:, 128 * c:128 * c + 128], 128, tkd[m], s.free)
                    tk = act(ATT[m % 2][:, :], s.ap[:, 0:TOK], ACT.Copy, last, ktfree[m % 2])
                    s.free = [tk]
                    turned.append((tk, last))
                if m == 0:
                    continue
                q = m - 1
                d_, f = q // 2, q % 2
                order = [4, 5, 0, 1, 2, 3] if d_ == 0 else [5, 4, 3, 2, 1, 0]
                KT = ATT[q % 2][:, :].rearrange("p (c e) -> p c e", e=128)
                ps_ = [pairs.take(), pairs.take()]
                for i, c in enumerate(order[:5]):
                    s = ps_[i // 4]
                    cc_ = 256 * (i % 4)
                    last = mm(s.ap[:, cc_:cc_ + 256], KT[:, c, :], V[:, c, 256 * f:256 * f + 256], i % 2 == 0, True,
                              turned[q][0], s.free, tv)
                ktfree[q % 2] = last
                tl = [tdec[q], tdec[q]]
                for i, c in enumerate(order[:5]):
                    s = ps_[i // 4]
                    nx = order[i + 1]
                    for hh in range(2):
                        rr = slice(64 * hh, 64 * hh + 64)
                        kv = s.ap[rr, 256 * (i % 4) + 128 * hh:256 * (i % 4) + 128 * hh + 128]
                        if i == 0:
                            tl[hh] = copy(S[rr, q, nx, :], kv, last, trs, [x for x in tb_])
                        else:
                            tl[hh] = stt(S[rr, q, nx, :], S[rr, q, c, :], DEC[rr, q, c:c + 1], kv, ALU.mult, ALU.add,
                                         tl[hh], tdec[q], last)
                    s.free = list(tl)
                tS.append(list(tl))
            for i in range(3):
                TR.slots[i].free = [turned[i][1] if i < 2 else w0]
            qbfree = [turned[2][1], turned[3][1]]
            attfree = list(ktfree)
            gfree = w0

            N = 128 * NC_
            jobs = [(d_, lv) for d_ in range(2) for lv in range(7)]

            def diffs(f, d_, lv):
                Bk = 2 << lv
                hb = Bk // 2
                x = TR.take()
                xv, bv = (y.rearrange("p (n s e) -> p n s e", s=2, e=hb) for y in
                          (x.ap[:, 0:N], B_[:, 2 * d_ + f, 0:N]))
                anc = (bv[:, :, 0, hb - 1:hb] if d_ == 0 else bv[:, :, 1, 0:1]).to_broadcast([128, N // Bk, hb])
                tq, sk = (1, 0) if d_ == 0 else (0, 1)
                ta = tt(xv[:, :, tq, :], bv[:, :, tq, :], anc, ALU.subtract, x.free, tb_)
                tb = tt(xv[:, :, sk, :], anc, bv[:, :, sk, :], ALU.subtract, x.free)
                return x, act(x.ap[:, 0:N], x.ap[:, 0:N], ACT.Exp, ta, tb), tb

            def factors(f, d_, lv, x, t):
                hb = 1 << lv
                tq, sk = (1, 0) if d_ == 0 else (0, 1)
                xv, qv, kv = (y.rearrange("p (n s e) -> p n s e", s=2, e=hb) for y in
                              (x.ap[:, 0:N], QK[:, f, 0:N], QK[:, 2 + f, 0:N]))
                z = ZK.take()
                tb = [None, None]
                for hh in (1, 0):
                    rr = slice(64 * hh, 64 * hh + 64)
                    zv = z.ap[hh][:, 0:N].rearrange("p (n s e) -> p n s e", s=2, e=hb)
                    tb[hh] = tt(zv[rr, :, sk, :], xv[rr, :, sk, :], kv[rr, :, sk, :], ALU.mult, t, z.free, tzk,
                                e="pool" if hh else "dve")
                ta = tt(xv[:, :, tq, :], xv[:, :, tq, :], qv[:, :, tq, :], ALU.mult, t)
                return x, z, ta, tb

            def products(x, z, ta, tb):
                ss_ = []
                for hh in range(2):
                    s = pairs.take()
                    for c in range(NC_):
                        cs = slice(128 * c, 128 * c + 128)
                        last = mm(s.ap[:, cs], z.ap[hh][:, cs], x.ap[:, cs], c % 4 == 0, True, ta, tb[hh], s.free)
                    ss_.append((s, last))
                x.free = z.free = [last]
                return ss_

            def place_level(tat, d_, lv, ss_):
                hb = 1 << lv
                tq = 1 if d_ == 0 else 0
                for hh, (s, last) in enumerate(ss_):
                    av, pv = (y.rearrange("p (n s e) -> p n s e", s=2, e=hb)[:, :, tq, :] for y in
                              (ATT[hh][:, 0:N], s.ap[:, 0:N]))
                    mv = MK[:, 7 * d_ + lv, 0:64 * NC_].rearrange("p (n e) -> p n e", e=hb)
                    tat[hh] = P.op("dve", lambda g, av=av, mv=mv, pv=pv: g.copy_predicated(av, mv, pv),
                                   last, tat[hh], tmk)
                    s.free = [tat[hh]]

            def finish(f, outs, G, tg_):
                free = []
                xs = []
                for hh in range(2):
                    o, last = outs[hh]
                    xs.append(act(QB[:, hh, 0:N], o.ap[:, 0:N], ACT.Square, last, outs[1][1]))
                for hh in range(2):
                    h = 2 * f + hh
                    o, last = outs[hh]
                    x = QB[:, hh, 0:N]
                    s, l2, _ = inverse_root([(QB[:, hh, :], xs[hh])], NC_, 1.0 / 128,
                                            lambda: take_not(outs[0][0], outs[1][0]))
                    t = act(x, s.ap[:, 0:N], ACT.Copy, l2)
                    s.free = [t]
                    t = stt(x, o.ap[:, 0:N], col(f"gla_o{L}"), x, ALU.mult, ALU.mult, t, last)
                    o.free = [t]
                    t = tt(G[hh], x, G[hh], ALU.mult, tg_[hh], t)
                    free.append(t)
                    ytok.append(split_into(Y4, h, G[hh], N, t))
                return free

            done = None
            ytok = []
            for f in range(2):
                e0, e1 = diffs(f, *jobs[0]), diffs(f, *jobs[1])
                tat = []
                for hh in range(2):
                    rr = slice(64 * hh, 64 * hh + 64)
                    s = take_not(*([done[1][0][0], done[1][1][0]] if done else []))
                    for c in range(NC_):
                        last = mm(s.ap[:, 128 * c:128 * c + 128], QK[rr, 2 + f, 128 * c:128 * c + 128],
                                  QK[rr, f, 128 * c:128 * c + 128], c % 4 == 0, True, s.free, tqk)
                    t = stt(ATT[hh][:, 0:N].rearrange("p (c e) -> p c e", e=128),
                            s.ap[:, 0:N].rearrange("p (c e) -> p c e", e=128), 2.0,
                            IDENT.unsqueeze(1).to_broadcast([128, NC_, 128]), ALU.mult, ALU.mult, last, attfree[hh])
                    s.free = [t]
                    tat.append(t)
                nxt = factors(f, *jobs[0], *e0[:2])
                if done:
                    qbfree = finish(*done)
                G = [place(n + f"g{f}{i}", [128, TOK], F32, (offY + 18432 + 3072 * i) if f == 0 else
                           offY2 + 6144 * i)[:, 0:N] for i in range(2)]
                tg_, tqb = [], []
                for i, (d_, lv) in enumerate(jobs):
                    ss_ = products(*nxt)
                    if i + 2 < len(jobs):
                        e2 = diffs(f, *jobs[i + 2])
                        if f == 0:
                            gnext = e2[1:]
                    if i + 1 < len(jobs):
                        nxt = factors(f, *jobs[i + 1], *e1[:2])
                        e1 = e2
                    place_level(tat, d_, lv, ss_)
                    if i in (4, 9):
                        gate_at = projB(xU, full)
                    if i in (5, 10):
                        hh = i // 10
                        s, last = gate_at
                        t1 = act(G[hh], s.ap[:, 0:N], ACT.Sigmoid, last, gfree)
                        t2 = tt(G[hh], G[hh], s.ap[:, 0:N], ALU.mult, t1)
                        s.free = [t2]
                        tg_.append(t2)
                    if i in (6, 11):
                        d2 = i // 11
                        t = act(QB[:, d2, 0:N], B_[:, 2 * d2 + f, 0:N], ACT.Exp, qbfree[d2])
                        tqb.append(tt(QB[:, d2, 0:N], QB[:, d2, 0:N], QK[:, f, 0:N], ALU.mult, t))
                outs = []
                for hh in range(2):
                    h = 2 * f + hh
                    rr = slice(64 * hh, 64 * hh + 64)
                    o = pairs.take()
                    for c in range(NC_):
                        cs = slice(128 * c, 128 * c + 128)
                        last = mm(o.ap[:, cs], V[:, c, 128 * h:128 * h + 128], ATT[hh][:, cs], c % 4 == 0, False,
                                  tat[hh], o.free, tv)
                        for d_ in range(2):
                            if c != (4 if d_ == 0 else 5):
                                last = mm(o.ap[:, cs], S[rr, 2 * d_ + f, c, :], QB[rr, d_, cs], False, False, tqb,
                                          tS[f], tS[2 + f])
                    outs.append((o, last))
                attfree = [last, last]
                gfree = [gnext, tqb]
                done = (f, outs, G, tg_)
            finish(*done)
            merge(True, full, f"g{L}", ytok, [attfree, [t for t in P.newest.values() if t.sem != "sp"]])

        def gqa(L, full):
            n = f"q{L}"
            N = TOK if full else LAT
            Q = place(n + "q", [128, 4, TOK], F32, offY2)
            G = place(n + "g", [128, 4, TOK], F32, offY2 + 12288)
            K = place(n + "k", [128, TOK], F32, offZ)
            V = place(n + "v", [128, 6, 128], F32, offZ + 3072)
            CS = place(n + "cs", [128, 2, 512], F32, offZ + 6144)
            RM = place(n + "rm", [128, 128], F32, offZ + 10240)
            o1 = offZ + 10752
            d1, d2 = dsem(), dsem()
            w0 = [t for t in P.newest.values() if t.sem != "sp"]
            tcs = [P.dma("sp", d1, CS[:, :, :], A["rope_q"], w0), P.dma("sp", d2, RM[:, :], A["rot_q"])]
            TS_ = Ring([Slot(place(n + f"t{i}", [128, TOK], F32, o1 + 3072 * i)[:, :]) for i in range(4)])
            scr = Ring([Slot(place(n + f"r{i}", [128, 512], F32, o1 + 12288 + 2048 * i)[:, :]) for i in range(2)])
            held = {}

            def silu_gate(j):
                s, last = projB(xU, full)
                x = TS_.take()
                t1 = act(x.ap[:, 0:N], s.ap[:, 0:N], ACT.Sigmoid, last, x.free)
                t2 = tt(G[:, j, 0:N], x.ap[:, 0:N], s.ap[:, 0:N], ALU.mult, t1)
                s.free = x.free = [t2]

            def proj_qk(j):
                f_ = full or j == 4
                s, last = projB(xU, f_)
                m = TOK if f_ else LAT
                z = Q[:, j, 0:m] if j < 4 else K[:, 0:m]
                t = act(z, s.ap[:, 0:m], ACT.Copy, last)
                s.free = [t]
                x = TS_.take()
                held[j] = (z, m, x, act(x.ap[:, 0:m], z, ACT.Square, t, x.free))

            def norm_qk(j):
                z, m, x, t = held[j]
                s = pairs.take()
                for a, b in (TG if m == TOK else TG[:1]):
                    last = mm(s.ap[:, a:b], BONES, x.ap[:, a:b], True, True, t, s.free)
                t = act(x.ap[:, 0:m], s.ap[:, 0:m], ACT.Sqrt, last, scale=1.0 / 64, bias=EPSC)
                s.free = [t]
                t = recip(x.ap[:, 0:m], x.ap[:, 0:m], t)
                t = stt(z, z, col(("qn" if j < 4 else "kn") + str(L)), x.ap[:, 0:m], ALU.mult, ALU.mult, t)
                x.free = [t]
                held[j] = (z, t)

            def turn_qk(j):
                z, t = held[j]
                return rope(z[:, 0:512], CS, RM[:, :], scr, [t, tcs])

            for n_ in range(7):
                if n_ < 5:
                    proj_qk(n_)
                elif n_ == 5:
                    ss, banks, last = projA(xU, 6, 128)
                    for i in range(6):
                        ss[i // 2].free = [copy(V[:, i, :], banks[i], last)]
                if n_ >= 6:
                    silu_gate(0)
                if 1 <= n_ < 6:
                    norm_qk(n_ - 1)
                if n_ >= 2:
                    turned = turn_qk(n_ - 2)
            KO = place(n + "ko", [128, TOK], F32, o1 + 16384)
            tko = odd_half(K[:, :], KO[:, :], turned)
            for j in range(1, 4):
                silu_gate(j)
            P.op("pe", None, tko, turned)
            P.barrier(free=("pe",))
            YT = Ring([Slot(place(n + f"y{i}", [128, 4, 128], F32, o1 + 19456 + 2048 * i)[:, :, :]) for i in range(2)])

            def qt(h, q0):
                return Q[:, h % 4, q0:q0 + 128]

            def kt(g, k0, m):
                return (KO if g else K)[:, k0:k0 + m]

            def ytile(q0, f, ap, last):
                y = YT.take()
                t = tt(y.ap, ap, G[:, :, q0:q0 + 128], ALU.mult, last, y.free)
                y.free = split(Y4[:, 0, 0:4, q0:q0 + 128], Y4[:, 1, 0:4, q0:q0 + 128], y.ap, t)
                ytok.append(y.free)
                return [t]
            ytok = []
            tiles = [(128 * j, [(0, 768, None)]) for j in range(4)]
            if full:
                tiles += [(512, [(512, 256, None)]), (640, [(512, 256, None)])]
            attention(n, 8, 2, qt, kt, lambda b, g: V[:, b, 64 * g:64 * g + 64], tiles, ytile, o1)
            merge(False, full, f"a{L}", [ytok] * 4, None)

        def sgu(L, full):
            n = f"u{L}"
            N = TOK if full else LAT
            NC_ = 6 if full else 4
            VN = place(n + "vn", [128, 6, 512], F32, offY2)
            LN = place(n + "ln", [128, 2, 512], F32, offY2 + 12288)
            WS_ = place(n + "w", [128, 4, 128], F32, offY2 + 16384)
            SB = place(n + "sb", [1, 4, 128], F32, offY2 + 18432)
            ST = place(n + "st", [128, 6, 8], F32, offY2 + 20480)
            d = [dsem() for _ in range(3)]
            w0 = [t for t in P.newest.values() if t.sem != "sp"]
            tl = [P.dma("sp", d[0], LN[:, :, :], A[f"sgu_ln{L}"].partition_broadcast(128), w0),
                  P.dma("sp", d[1], WS_[:, :, :], A[f"sgu_w{L}"]),
                  P.dma("sp", d[2], SB[:, :, :], A[f"sgu_b{L}"])]
            ss, banks, last = projA(xU, NC_, 512)
            tvn, ytok = [], []
            for i in range(NC_):
                t = P.op("dve", lambda g, i=i: g.bn_stats(ST[:, i, 0:6], banks[i]), last)
                t = P.op("dve", lambda g, i=i: g.bn_aggr(ST[:, i, 6:8], ST[:, i, 0:6]), t)
                t1 = act(ST[:, i, 0:1], ST[:, i, 7:8], ACT.Sqrt, t, bias=EPSC)
                t1 = recip(ST[:, i, 0:1], ST[:, i, 0:1], t1)
                t = ts(VN[:, i, :], banks[i], ST[:, i, 6:7], ST[:, i, 0:1], ALU.subtract, ALU.mult, t1, t)
                ss[i // 2].free = [t]
                t = tt(VN[:, i, :], VN[:, i, :], LN[:, 0, :], ALU.mult, t, tl)
                tvn.append(tt(VN[:, i, :], VN[:, i, :], LN[:, 1, :], ALU.add, t))
            T = Ring([Slot(place(n + f"t{i}", [128, TOK], F32, offZ + 3072 * i)[:, :]) for i in range(6)])

            def gates(g):
                s, last = projB(xU, full)
                x = T.take()
                tx = act(x.ap[:, 0:N], s.ap[:, 0:N], ACT.Copy, last, x.free)
                s.free = [tx]
                s, last = projB(xU, full)
                y = T.take()
                t = act(y.ap[:, 0:N], s.ap[:, 0:N], ACT.Sigmoid, last, y.free)
                t = tt(y.ap[:, 0:N], y.ap[:, 0:N], s.ap[:, 0:N], ALU.mult, t)
                s.free = [t]
                t = tt(x.ap[:, 0:N], x.ap[:, 0:N], y.ap[:, 0:N], ALU.mult, t, tx)
                y.free = [t]
                return x, t

            nxt = gates(0)
            for g in range(4):
                x, t = nxt
                if g < 3:
                    nxt = gates(g + 1)
                s = pairs.take()
                for c in range(NC_):
                    mm(s.ap[:, 128 * c:128 * c + 128], VN[:, c, 128 * g:128 * g + 128], WS_[:, g, :], c % 4 == 0, False,
                       s.free, tl, tvn)
                    last = mm(s.ap[:, 128 * c:128 * c + 128], ONES[0:1, :], SB[0:1, g, :], False, False)
                t = tt(x.ap[:, 0:N], x.ap[:, 0:N], s.ap[:, 0:N], ALU.mult, t, last)
                s.free = [t]
                x.free = split_into(Y4, g, x.ap[:, 0:N], N, t)
                ytok.append(x.free)
            merge(False, full, f"s{L}", ytok, ytok)

        if stop is None or stop.startswith("b"):
            sr, tr_ = root(False)
            tH = []
            for k in range(8):
                tH.append([tctx, stt(HT[:, k, 0:512], HT[:, k, 0:512], col("final_norm", k), sr.ap[:, 0:512], ALU.mult, ALU.mult, tr_)])
            sr.free = [tH[-1][1]]
            xs_sem, xl_sems = dsem(), [dsem() for _ in range(2)]
            for L in range(2):
                full = L == 0
                N = TOK if full else LAT
                cur[0] = 2 + L
                for v in range(2):
                    tg = ts(MU[:, 8 * v:8 * v + 8], modall(1, v), 1.0, None, ALU.add, None)
                T1 = Ring([Slot(place(f"un{L}{i}", [128, TOK], F32, offZ + 3072 * i)[:, :]) for i in range(4)])
                ready = []
                prev = None
                for k in range(9):
                    if k < 8:
                        a = T1.take()
                        tl = [ts(a.ap[:, lo:hi_], HT[:, k, lo:hi_], MU[:, 8 * v + k:8 * v + k + 1], mod(0, k, v),
                                 ALU.mult, ALU.add, tH[k], tg, a.free) for lo, hi_, v in groups(True)]
                        th = act(U[:, 0, k, :], a.ap, ACT.Copy, tl)
                    if prev is not None:
                        pa, ph = prev
                        pa.free = [ph, tt(U[:, 1, k - 1, :], pa.ap, U[:, 0, k - 1, :].bitcast(F32), ALU.subtract, ph)]
                        ready.append(pa.free)
                    prev = (a, th)
                tXS = P.dma("sp", xs_sem, XS, HT, [t for t in P.newest.values() if t.sem != "sp"], tH)
                P.barrier(free=("pe",))
                gla(L, full, ready)
                if stop == f"bg{L}":
                    break
                gqa(L, full)
                if stop == f"bq{L}":
                    break
                sgu(L, full)
                if stop == f"bs{L}":
                    break
                tu = [split(U[:, 0, k, 0:N], U[:, 1, k, 0:N], HT[:, k, 0:N]) for k in range(8)]
                P.barrier(free=("pe",))
                X = Ring([Slot(place(f"xl{L}{i}", [128, TOK], F32, offZ + 3072 * i)[:, :]) for i in range(2)])
                w0 = [t for t in P.newest.values() if t.sem != "sp"]
                for k in range(8):
                    x = X.take()
                    tx = P.dma("sp", xl_sems[k % 2], x.ap[:, 0:N], XS[:, k, 0:N], x.free, w0, tXS)
                    s, last = projB(xU, full, xt=tu if k == 0 else None)
                    tl = []
                    for lo, hi_, v in groups(full):
                        tl.append(ts(HT[:, k, lo:hi_], s.ap[:, lo:hi_], mod(2, k, v), None, ALU.mult, None, last))
                    s.free = tl
                    t = stt(HT[:, k, 0:N], x.ap[:, 0:N], ALPHA, HT[:, k, 0:N], ALU.mult, ALU.add, tl, tx)
                    x.free = [t]
                    if k == 0:
                        acc[0] = act(ACC[:, 0:N], HT[:, 0, 0:N], ACT.Copy, t)
                    else:
                        acc[0] = tt(ACC[:, 0:N], ACC[:, 0:N], HT[:, k, 0:N], ALU.add, t, acc[0], e="pool")
                MEAN = place(f"lm{L}", [128, TOK], F32, offZ + 15360)
                s = pairs.take()
                for a, b in (TG if full else TG[:1]):
                    last = mm(s.ap[:, a:b], ONES, ACC[:, a:b], True, True, acc[0], s.free)
                t = act(MEAN[:, 0:N], s.ap[:, 0:N], ACT.Copy, last, scale=1.0 / D)
                s.free = [t]
                t2 = [tt(HT[:, k, 0:N], HT[:, k, 0:N], MEAN[:, 0:N], ALU.subtract, t, last) for k in range(8)]
                LS = [place(f"ls{L}{k}", [128, TOK], F32, offZ + 18432 + 3072 * k) for k in range(4)]
                LS += [place(f"ls{L}{k}", [128, TOK], F32, offY + 3072 * k) for k in range(4, 8)]
                srcs = [(LS[k], act(LS[k][:, 0:N], HT[:, k, 0:N], ACT.Square, t2[k], last)) for k in range(8)]
                sr, t, _ = inverse_root(srcs, N // 128, 1.0 / D)
                tH = []
                for k in range(8):
                    t2 = tt(HT[:, k, 0:N], HT[:, k, 0:N], sr.ap[:, 0:N], ALU.mult, t)
                    tH.append(act(HT[:, k, 0:N], HT[:, k, 0:N], ACT.Identity, t2, scale=col(f"post_g{L}", k),
                                  bias=col(f"post_b{L}", k)))
                sr.free = [t2]
                if stop == f"b{L}":
                    break

        osem = [dsem() for _ in range(2)]
        OUT = [place(f"out{i}", [128, 1024], F32, offZ + 4096 * i) for i in range(2)]
        P.barrier()
        tod = [None, None]
        for i in range(4):
            s = pairs.take()
            for k in range(8):
                last = tr(s.ap[:, 128 * k:128 * k + 128], HT[:, k, 128 * i:128 * i + 128], 128, s.free)
            o = OUT[i % 2]
            t = copy(o[:, :], s.ap, last, tod[i % 2])
            s.free = [t]
            tod[i % 2] = P.dma("sp", osem[i % 2], out[0, 128 * i:128 * i + 128, :], o[:, :], t)
        P.op("sp", None, tod)

        P.number()
        block = ctx.enter_context(nc.Block())

        @block.sync
        def _(eng):
            P.emit("sp", eng, sems)

        @block.tensor
        def _(eng):
            P.emit("pe", eng, sems)

        @block.scalar
        def _(eng):
            P.emit("act", eng, sems)

        @block.vector
        def _(eng):
            P.emit("dve", eng, sems)

        @block.gpsimd
        def _(eng):
            P.emit("pool", eng, sems)


def _tiles_b(w):
    k, n = w.shape
    return np.ascontiguousarray(w.reshape(k // 128, 128, n // 128, 128).transpose(2, 1, 0, 3)).reshape(n // 128, 128, k)


def _tiles_a(w, n):
    nk = 1024 // n
    g = w.shape[1] // n
    return np.ascontiguousarray(w.reshape(8 // nk, nk, 128, g, n).transpose(3, 0, 2, 1, 4)).reshape(-1, 128, 1024)


def _tiles_br(w):
    return np.ascontiguousarray(w.reshape(4, 128, 4, 256).transpose(2, 1, 0, 3)).reshape(4, 128, 1024)


def _w2(w):
    return np.concatenate([_tiles_b(w[1024 * g:1024 * g + 1024]) for g in range(4)])


def _pad(w, pieces):
    out = np.zeros((w.shape[0], 128), w.dtype)
    for at, a, b in pieces:
        out[:, at:at + b - a] = w[:, a:b]
    return out


def _feat(x):
    return np.ascontiguousarray(x.T.reshape(8, 128, -1).transpose(1, 0, 2))


def _heads(w, order):
    return np.concatenate([w[:, 64 * h:64 * h + 64] for h in order], 1)


def _constants():
    f = np.float32
    p = np.arange(128)
    cm = np.zeros((128, 648), f)
    cm[:, 0:128] = np.eye(128)
    cm[:, 128:256] = 1
    cm[:, 256:384] = (p[:, None] // 64) == (p[None, :] // 64)
    cm[:, 384:512] = np.where(p[None, :] >= p[:, None], 0, NEG)
    cm[:, 512:640] = np.where(p[None, :] <= p[:, None], 0, NEG)
    cm[0:2, 640] = 1
    cm[2:4, 641] = 1
    t = np.arange(LAT)
    row, col = (t // 64).astype(f), (t % 64).astype(f)
    inv = (f(10000.0) ** (-np.arange(16, dtype=f) / f(16))).astype(f)
    ar, ac = (row[:, None] * inv).astype(f), (col[:, None] * inv).astype(f)
    a_s = np.concatenate([ar, ac], 1)[:, p % 32].T
    a_q = np.where(((p % 64) < 32)[:, None], ar[:, p % 16].T, ac[:, p % 16].T)
    rope = [np.stack([np.cos(a), np.sin(a)], 1).astype(f) for a in (a_s, a_q)]
    rot = []
    for half in (32, 16):
        r = np.zeros((128, 128), f)
        for m in range(128):
            if m % (2 * half) < half:
                r[m + half, m] = -1
            else:
                r[m - half, m] = 1
        rot.append(r)
    gm = np.zeros((128, 14, 6, 64), np.uint8)
    for lv in range(7):
        b = 2 << lv
        h = b // 2
        c = np.arange(64)
        blk = c // h
        same = (p[:, None] // b) == blk[None, :]
        gm[:, lv] = (same & ((p[:, None] % b) < h))[:, None, :]
        gm[:, 7 + lv] = (same & ((p[:, None] % b) >= h))[:, None, :]
    rs = np.ones((128, 2, TOK), f)
    rs[:, 0, 0::128] = 0
    rs[:, 1, 127::128] = 0
    return {"cmat": cm, "rope_s": rope[0], "rope_q": rope[1], "rot_s": rot[0], "rot_q": rot[1],
            "gmask": gm.reshape(128, 14, 384).view(np.int32), "reset": rs}


def layout(I):
    I = {k: np.asarray(v) for k, v in I.items()}
    f = np.float32
    A = dict(_constants())
    A["hT"] = _feat(np.concatenate([I["x"][0], I["ctx"][0]]))
    A["ctx2T"] = _feat(I["ctx_2"][0])
    cols = np.zeros((128, NCOLS), f)

    def put(name, v):
        a, n = COLS[name]
        cols[:, a:a + n] = v.reshape(n, 128).T
    for L in range(2):
        put(f"ada_b{L}", I["ada_b"][L])
        put(f"ada2_b{L}", I["b_ada_2"][L])
        put(f"norm_mix{L}", I["norm_mix"][L])
        put(f"norm_ffn{L}", I["norm_ffn"][L])
        put(f"post_g{L}", I["post_ln_g_2"][L])
        put(f"post_b{L}", I["post_ln_b_2"][L])
        put(f"gla_o{L}", I["gla_o_norm_2"][L])
        put(f"abf{L}", I["gla_ab_f_2"][L])
        put(f"abb{L}", I["gla_ab_b_2"][L])
        put(f"qn{L}", np.concatenate([I["attn_q_norm_2"][L]] * 2))
        put(f"kn{L}", np.concatenate([I["attn_k_norm_2"][L]] * 2))
    put("head_norm", I["mlstm_head_norm"][0])
    put("final_norm", I["final_norm"])
    gb = I["mlstm_gate_b"][0]
    for name, (a, b) in (("gb_i", (0, 2)), ("gb_f", (1, 3))):
        c = COLS[name][0]
        cols[0:8, c] = gb[a]
        cols[32:40, c] = gb[b]
    c0 = COLS["cond"][0]
    for b, (u, v) in enumerate(((I["c"][0], I["c_ctx"]), (I["c_2"][0], I["c_ctx_2"]))):
        for j, x in enumerate((u, v)):
            cols[:, c0 + 16 * b + j:c0 + 16 * b + 16:2] = x.reshape(8, 128).T
    a, n = COLS["sink"]
    cols[:, a:a + n] = I["swa_sink"][0][None, :]
    A["cols"] = cols
    w = I["mlstm_w_in"][0]
    A["mqk"] = _tiles_b(w[:, 0:1024])
    A["mv"] = _tiles_a(w[:, 1024:2048], 512)
    A["mo"] = _tiles_b(w[:, 2048:3072])
    g = w[:, 3072:3104]
    A["mgate"] = _tiles_b(_pad(g, [(0, 0, 8), (32, 16, 24), (64, 8, 16), (96, 24, 32)]))
    A["mout"] = _tiles_b(I["mlstm_w_out"][0])
    w = I["swa_w_in"][0]
    order = [0, 4, 1, 5, 2, 6, 3, 7, 8, 12, 9, 13, 10, 14, 11, 15]
    A["sqk"] = _tiles_b(np.concatenate([_heads(w[:, 0:1024], order), w[:, 1024:1280]], 1))
    A["sv"] = _tiles_a(w[:, 1280:1536], 256)
    A["sout"] = _tiles_b(I["swa_w_out"][0])
    for L in range(2):
        A[f"ada{L}"] = _tiles_a(I["ada_w"][L], 512)
        A[f"w1_{L}"] = _tiles_b(I["ffn_w1"][L])
        A[f"w2_{L}"] = _w2(I["ffn_w2"][L])
        A[f"adb{L}"] = _tiles_a(I["w_ada_2"][L], 512)
        w = I["w_in_2"][L]
        A[f"p_aqk{L}"] = _tiles_b(np.concatenate([_heads(w[:, 0:512], [0, 4, 1, 5, 2, 6, 3, 7]), w[:, 512:640]], 1))
        A[f"p_av{L}"] = _tiles_a(w[:, 640:768], 128)
        A[f"p_ag{L}"] = _tiles_b(w[:, 768:1280])
        A[f"p_gqk{L}"] = _tiles_b(w[:, 1280:1792])
        A[f"p_gv{L}"] = _tiles_a(w[:, 1792:2304], 512)
        A[f"p_gate{L}"] = _tiles_b(_pad(w, [(0, 2304, 2320), (32, 2320, 2336)]))
        A[f"p_gg{L}"] = _tiles_b(w[:, 2336:2848])
        A[f"p_su{L}"] = _tiles_b(w[:, 2848:3360])
        A[f"p_sv{L}"] = _tiles_a(w[:, 3360:3872], 512)
        A[f"p_sg{L}"] = _tiles_b(w[:, 3872:4384])
        A[f"p_ma{L}"] = _tiles_b(w[:, 4384:5408])
        A[f"p_mg{L}"] = _tiles_b(w[:, 5408:6432])
        A[f"p_ms{L}"] = _tiles_b(w[:, 6432:7456])
        A[f"br_a{L}"] = _tiles_br(I["w_br_attn_2"][L])
        A[f"br_g{L}"] = _tiles_br(I["w_br_gla_2"][L])
        A[f"br_s{L}"] = _tiles_br(I["w_br_sgu_2"][L])
        A[f"wo{L}"] = _tiles_b(I["w_out_2"][L])
        a2 = np.zeros((64, 256), f)
        a2[0:16] = I["gla_a2_f_2"][L]
        a2[32:48] = I["gla_a2_b_2"][L]
        A[f"a2_{L}"] = a2
        A[f"sgu_ln{L}"] = np.stack([I["sgu_ln_g_2"][L], I["sgu_ln_b_2"][L]])
        A[f"sgu_w{L}"] = np.ascontiguousarray(I["sgu_w_2"][L].transpose(2, 0, 1))
        A[f"sgu_b{L}"] = np.ascontiguousarray(I["sgu_b_2"][L].reshape(1, 4, 128))
    return A


def kernel(**inputs):
    import concourse.bacc as _bacc
    from concourse.bass_utils import run_bass_kernel_spmd as _run

    nc = _bacc.Bacc("TRN2", target_bir_lowering=False, num_devices=1)
    arrays, A = {}, {}
    for name, a in layout(inputs).items():
        arrays[f"in_{name}"] = a
        A[name] = nc.dram_tensor(f"in_{name}", a.shape, mybir.dt.from_np(a.dtype), kind="ExternalInput").ap()
    out = nc.dram_tensor("out_x", (1, LAT, D), F32, kind="ExternalOutput").ap()
    trunk_kernel(nc, A, out)
    r = _run(nc, [arrays], core_ids=[0])
    return r.results[0]["out_x"]
```
